# Optimizing a Trainium2 kernel written in Bass

```python
import jax, jax.numpy as jnp
from jax import lax
import numpy as np

D_MODEL = 2048
BATCH = 1
SEQ = 512
DEPTH = 1

D_MIX = D_MODEL
D_LRU = D_MIX // 2
N_LRU_BLOCKS = 16
LRU_BLOCK = D_LRU // N_LRU_BLOCKS
CONV_WIDTH = 4
LRU_C = 8.0
D_ATT = D_MIX - D_LRU
ATT_HEAD_DIM = 128
N_ATT_HEADS = D_ATT // ATT_HEAD_DIM
Q_BLOCK = 128
D_FF = 4 * D_MODEL
N_MOD = 6
EPS = 1e-6
D_IN_PROJ = 2 * D_LRU + 3 * D_ATT + N_ATT_HEADS

kernel_name = "hymba_rglru_fox_sandwich_adaln"

def rms_norm(x, g):
    xf = x.astype(jnp.float32)
    y = xf * lax.rsqrt(jnp.mean(jnp.square(xf), axis=-1, keepdims=True) + EPS)
    return (y * g.astype(jnp.float32)).astype(x.dtype)

def modulate(h, shift, scale):
    return h * (1 + scale[:, None, :]) + shift[:, None, :]

def causal_depthwise_conv(u, w, b):
    C = u.shape[-1]
    out = lax.conv_general_dilated(
        u, w[:, None, :], window_strides=(1,), padding=[(CONV_WIDTH - 1, 0)],
        dimension_numbers=("NWC", "WIO", "NWC"), feature_group_count=C)
    return out + b

def rg_lru(xc, w_rg, b_rg, w_ig, b_ig, lam):
    B, S, C = xc.shape
    xb = xc.reshape(B, S, N_LRU_BLOCKS, LRU_BLOCK)
    r = jax.nn.sigmoid(jnp.einsum("bsni,nij->bsnj", xb, w_rg).reshape(B, S, C) + b_rg)
    i = jax.nn.sigmoid(jnp.einsum("bsni,nij->bsnj", xb, w_ig).reshape(B, S, C) + b_ig)
    log_a = -LRU_C * r.astype(jnp.float32) * jax.nn.softplus(-lam.astype(jnp.float32))
    a = jnp.exp(log_a)
    mult = jnp.sqrt(-jnp.expm1(2.0 * log_a))
    bx = mult * (i * xc).astype(jnp.float32)

    def combine(left, right):
        a1, b1 = left
        a2, b2 = right
        return a1 * a2, a2 * b1 + b2

    _, h = lax.associative_scan(combine, (a, bx), axis=1)
    return h.astype(xc.dtype)

def fox_attention(q, k, v, log_f):
    B, S, H, Dh = q.shape
    n_blocks = S // Q_BLOCK
    F = jnp.cumsum(log_f, axis=1).transpose(0, 2, 1)
    qb = q.reshape(B, n_blocks, Q_BLOCK, H, Dh).transpose(1, 0, 2, 3, 4)
    Fq = F.reshape(B, H, n_blocks, Q_BLOCK).transpose(2, 0, 1, 3)
    key_pos = jnp.arange(S)
    scale = Dh ** -0.5

    def attend_block(args):
        qi, Fi, blk = args
        s = jnp.einsum("bqhd,bkhd->bhqk", qi, k, preferred_element_type=jnp.float32) * scale
        bias = Fi[..., :, None] - F[..., None, :]
        q_pos = blk * Q_BLOCK + jnp.arange(Q_BLOCK)
        causal = key_pos[None, :] <= q_pos[:, None]
        logits = jnp.where(causal, s + bias, -jnp.inf)
        p = jax.nn.softmax(logits, axis=-1)
        return jnp.einsum("bhqk,bkhd->bqhd", p.astype(v.dtype), v)

    out = lax.map(attend_block, (qb, Fq, jnp.arange(n_blocks)))
    return out.transpose(1, 0, 2, 3, 4).reshape(B, S, H, Dh)

def setup_inputs(seed: int = 0) -> dict:
    key = jax.random.key(seed)
    ks = jax.random.split(key, 24)
    L, D = DEPTH, D_MODEL
    nrm = jax.random.normal

    def gain(k, n):
        return 1.0 + 0.05 * nrm(k, (L, n), jnp.float32)

    a0 = jax.random.uniform(ks[12], (L, D_LRU), jnp.float32, minval=0.9, maxval=0.999)
    return {
        "x": nrm(ks[0], (BATCH, SEQ, D), jnp.float32),
        "c": nrm(ks[1], (BATCH, D), jnp.float32),
        "w_ada": 0.5 * nrm(ks[2], (L, D, N_MOD * D), jnp.float32) * D ** -0.5,
        "b_ada": 0.01 * nrm(ks[3], (L, N_MOD * D), jnp.float32),
        "g_pre_mix": gain(ks[4], D),
        "g_post_mix": gain(ks[5], D),
        "g_pre_mlp": gain(ks[6], D),
        "g_post_mlp": gain(ks[7], D),
        "w_in": nrm(ks[8], (L, D, D_IN_PROJ), jnp.float32) * D ** -0.5,
        "conv_w": nrm(ks[9], (L, CONV_WIDTH, D_LRU), jnp.float32) * CONV_WIDTH ** -0.5,
        "conv_b": 0.01 * nrm(ks[10], (L, D_LRU), jnp.float32),
        "w_rg": nrm(ks[11], (L, N_LRU_BLOCKS, LRU_BLOCK, LRU_BLOCK), jnp.float32) * LRU_BLOCK ** -0.5,
        "b_rg": 0.01 * nrm(ks[13], (L, D_LRU), jnp.float32),
        "w_ig": nrm(ks[14], (L, N_LRU_BLOCKS, LRU_BLOCK, LRU_BLOCK), jnp.float32) * LRU_BLOCK ** -0.5,
        "b_ig": 0.01 * nrm(ks[15], (L, D_LRU), jnp.float32),
        "lru_lambda": jnp.log(a0) - jnp.log1p(-a0),
        "b_forget": jax.random.uniform(ks[16], (L, N_ATT_HEADS), jnp.float32, minval=1.0, maxval=4.0),
        "g_lru_out": gain(ks[17], D_LRU),
        "g_att_out": gain(ks[18], D_ATT),
        "w_out": nrm(ks[19], (L, D_MIX, D), jnp.float32) * D_MIX ** -0.5,
        "w_ff1": nrm(ks[20], (L, D, D_FF), jnp.float32) * D ** -0.5,
        "w_ff2": nrm(ks[21], (L, D_FF, D), jnp.float32) * D_FF ** -0.5,
    }

def reference(x, c, w_ada, b_ada, g_pre_mix, g_post_mix, g_pre_mlp, g_post_mlp, w_in, conv_w, conv_b,
              w_rg, b_rg, w_ig, b_ig, lru_lambda, b_forget, g_lru_out, g_att_out, w_out, w_ff1, w_ff2):
    B, S, _ = x.shape
    c_act = jax.nn.silu(c)
    split_at = [D_LRU, 2 * D_LRU, 2 * D_LRU + D_ATT, 2 * D_LRU + 2 * D_ATT, 2 * D_LRU + 3 * D_ATT]
    for l in range(DEPTH):
        mod = c_act @ w_ada[l] + b_ada[l]
        sh1, sc1, gt1, sh2, sc2, gt2 = jnp.split(mod, N_MOD, axis=-1)

        h = modulate(rms_norm(x, g_pre_mix[l]), sh1, sc1)
        proj = h @ w_in[l]
        u_lru, u_gate, q, k, v, f_logit = jnp.split(proj, split_at, axis=-1)

        xc = causal_depthwise_conv(u_lru, conv_w[l], conv_b[l])
        y_lru = rg_lru(xc, w_rg[l], b_rg[l], w_ig[l], b_ig[l], lru_lambda[l]) * jax.nn.gelu(u_gate)

        q = q.reshape(B, S, N_ATT_HEADS, ATT_HEAD_DIM)
        k = k.reshape(B, S, N_ATT_HEADS, ATT_HEAD_DIM)
        v = v.reshape(B, S, N_ATT_HEADS, ATT_HEAD_DIM)
        log_f = jax.nn.log_sigmoid((f_logit + b_forget[l]).astype(jnp.float32))
        y_att = fox_attention(q, k, v, log_f).reshape(B, S, D_ATT)

        y = jnp.concatenate([rms_norm(y_lru, g_lru_out[l]), rms_norm(y_att, g_att_out[l])], axis=-1) @ w_out[l]
        x = x + gt1[:, None, :] * rms_norm(y, g_post_mix[l])

        h = modulate(rms_norm(x, g_pre_mlp[l]), sh2, sc2)
        y = jnp.square(jax.nn.relu(h @ w_ff1[l])) @ w_ff2[l]
        x = x + gt2[:, None, :] * rms_norm(y, g_post_mlp[l])
    return x


_drawn_inputs = setup_inputs


def setup_inputs(seed=0):
    import zlib

    import numpy as np

    out = dict(_drawn_inputs(seed))
    spreads = {}
    factors = {'b_ada': 3.546,
     'g_pre_mix': 3.179,
     'g_post_mix': 3.594,
     'g_pre_mlp': 3.634,
     'g_post_mlp': 3.89,
     'conv_b': 8.0,
     'b_rg': 57.955,
     'b_ig': 48.554,
     'g_lru_out': 5.506,
     'g_att_out': 5.555}
    for name, (base, spread) in spreads.items():
        noise = np.random.default_rng([zlib.crc32(name.encode()), seed]).standard_normal(out[name].shape)
        drawn = base * np.exp(spread * noise) if base else spread * noise
        out[name] = __import__('jax').numpy.asarray(drawn.astype(out[name].dtype))
    for name, factor in factors.items():
        out[name] = (out[name] * factor).astype(out[name].dtype)
    return out
```

```python
from contextlib import ExitStack

import concourse.bass as bass
from concourse import mybir

F32 = mybir.dt.float32
F32R = mybir.dt.float32r
ALU = mybir.AluOpType
ACT = mybir.ActivationFunctionType
AX = mybir.AxisListType.X

P = 128
EPS = 1e-6
LRU_C = 8.0
MASKED = -1e30
RING = 4
COLS = 512
LAG = 3


def hybrid_layer(nc, x, c, w_ada, b_ada, g_pre_mix, g_post_mix, g_pre_mlp, g_post_mlp, w_in, conv_w, conv_b,
                 w_rg, b_rg, w_ig, b_ig, lru_lambda, b_forget, g_lru_out, g_att_out, w_out, w_ff1, w_ff2, out):
    S, D = x.shape[1], x.shape[2]
    D_LRU, D_ATT, D_FF = conv_b.shape[1], g_att_out.shape[1], w_ff1.shape[2]
    HEADS = b_forget.shape[1]
    DH = D_ATT // HEADS
    CW = conv_w.shape[1]
    LB = w_rg.shape[2]
    KT = D // P
    NT = S // P
    CT = D_LRU // P
    CHUNKS = 8
    FT = D_FF // CHUNKS // P
    assert (S, D, DH, KT, NT, CT, FT, CW, HEADS, LB) == (512, 2048, 128, 16, 4, 8, 8, 4, 8, 64)

    x2 = x.rearrange("b s d -> (b s) d")
    out2 = out.rearrange("b s d -> (b s) d")
    w_ada2, w_in2, w_out2, w_ff12, w_ff22 = (w.rearrange("l k n -> (l k) n") for w in (w_ada, w_in, w_out, w_ff1, w_ff2))

    U_LAST = 2 * KT // 2
    U_PROJ = U_LAST + 2
    U_ATT = U_PROJ + 8 * 8
    U_OUT = U_ATT + HEADS
    U_MLP = U_OUT + 24
    PER_CHUNK = 32
    U_LOOP = U_MLP + PER_CHUNK
    REST = [(2, 0), (0, 1), (1, 1), (2, 1), (3, 0), (3, 1)]

    def ada_after(n):
        if U_PROJ <= n < U_ATT:
            return 1 + (n >= U_ATT - 8)
        return 2 * (U_OUT + 3 <= n < U_OUT + 15 or U_MLP + 8 <= n < U_MLP + 24)

    stream, main_pos, ada_pos, ada_of = [], {}, {}, {}
    for n in range(U_LOOP):
        main_pos[n] = len(stream)
        stream.append(("w", n))
        ada_of[n] = []
        for _ in range(ada_after(n)):
            a = len(ada_pos)
            ada_of[n].append(a)
            ada_pos[a] = len(stream)
            stream.append(("ada", a))
    POS_LOOP = len(stream)
    assert len(ada_pos) == 16 * 8 and PER_CHUNK % RING == 0
    COLUMNS_AT = {1: 6, 2: 4, 3: 4, 4: 4, 5: 4, 6: 4, 7: 2}
    ADA_COL = [base * D + g * COLS for base in (4, 3, 2, 5) for g in range(4)]

    def place(pos):
        return pos % RING, 16 * (pos // RING + 1)

    def chunk_raw(ck, j):
        if isinstance(ck, int) and ck == 0:
            return place(main_pos[U_MLP + j])
        slot, count = place(POS_LOOP + j)
        return slot, count + (ck - 1) * (16 * PER_CHUNK // RING)

    def unit(n):
        return (*place(main_pos[n]), n % RING)

    def lo_count(n):
        return n // 2 + 1 if n < U_LAST else n - 7

    with ExitStack() as ctx:
        def sb(name, shape, dt=F32):
            return ctx.enter_context(nc.sbuf_tensor(name, shape, dt))

        def sem(name):
            return ctx.enter_context(nc.semaphore(name))

        def overlay(*specs):
            with ExitStack() as phase:
                return [phase.enter_context(nc.sbuf_tensor(n, s, d)) for n, s, d in specs]

        raw = sb("raw", [P, RING, 2 * COLS])
        w_hi = sb("w_hi", [P, RING, 2 * COLS], F32R)
        w_lo = sb("w_lo", [P, RING, 2 * COLS], F32R)
        ident = sb("ident", [P, P])
        ones = sb("ones", [P, P])
        causal = sb("causal", [P, P])
        vrow = sb("vrow", [P, P])
        vcol = sb("vcol", [P, 112])
        acc = sb("acc", [P, 2, COLS])
        acc_init = sb("acc_init", [P, COLS])
        g_row = sb("g_row", [P, COLS])
        ssq = sb("ssq", [P, COLS])
        cc = sb("cc", [P, 4, KT])
        A1, S1, A2, S2 = (sb(n, [P, KT]) for n in ("A1", "S1", "A2", "S2"))
        stat = sb("stat", [P, 96])
        lam = sb("lam", [P, 8, CT])
        wf_raw = sb("wf_raw", [P, KT, HEADS])
        bf = sb("bf", [HEADS, 1])
        eps = sb("eps", [P, 1])

        G_PRE_MIX, G_PRE_MLP, CONVW, CONVB, B_RG, B_IG, LAMBDA, G_LRU, G_ATT = 0, 16, 32, 64, 72, 80, 88, 96, 104

        h_hi, x_tok, gst0, xnT, gst1, junk, xdiag = overlay(
            ("h_hi", [P, KT, COLS], F32R), ("x_tok", [P, NT, D], F32), ("gst0", [P, 8, 2, 256], F32),
            ("xnT", [P, KT, COLS], F32), ("gst1", [P, 8, 2, 256], F32), ("junk", [P, D], F32), ("xdiag", [P, NT, P], F32))
        _, h_lo, hs, rg, ig, ut, wrg, wig, a_sq, sq = overlay(
            ("pad2", [P, KT, COLS], F32), ("h_lo", [P, KT, COLS], F32R), ("hs", [P, CT, COLS], F32),
            ("rg", [P, CT, COLS], F32), ("ig", [P, CT, COLS], F32), ("ut", [P, CT, COLS], F32),
            ("wrg", [P, CT, P], F32), ("wig", [P, CT, P], F32), ("a_sq", [P, 2, COLS], F32), ("sq", [P, COLS], F32))
        yl_hi, yl_lo, ya_hi, ya_lo, yacc, qT, kT, vv, LP, PT, nF, nFm = overlay(
            ("yl_hi", [P, CT, COLS], F32R), ("yl_lo", [P, CT, COLS], F32R), ("ya_hi", [P, HEADS, COLS], F32R),
            ("ya_lo", [P, HEADS, COLS], F32R), ("yacc", [P, NT, 2, COLS], F32), ("qT", [P, HEADS, S], F32),
            ("kT", [P, HEADS, S], F32), ("vv", [P, NT, D_ATT], F32), ("LP", [P, 1280], F32), ("PT", [P, 1280], F32),
            ("nF", [P, 2, S], F32), ("nFm", [P, S], F32))
        *_, wf_hi, wf_lo = overlay(("pad3", [P, 128 * 256], F32), ("wf_hi", [P, KT, P], F32R), ("wf_lo", [P, KT, P], F32R))
        _, xr, yg, G1, xr2, x1diag, junk2, mtmp = overlay(
            ("pad4", [P, 64 * 256], F32), ("xr", [P, 2, D], F32), ("yg", [P, NT, D], F32), ("G1", [P, D], F32),
            ("xr2", [P, D], F32), ("x1diag", [P, NT, P], F32), ("junk2", [P, D], F32), ("mtmp", [P, 2, COLS], F32))
        x1r, _, u_hi, _, u_lo, G2, rt, u_full_t, junk3 = overlay(
            ("x1r", [P, NT, D], F32), ("pad5", [P, 32 * 256], F32), ("u_hi", [P, FT, COLS], F32R),
            ("pad6", [P, 32 * 256], F32), ("u_lo", [P, FT, COLS], F32R), ("G2", [P, D], F32),
            ("rt", [P, 2, COLS], F32), ("u_full_t", [P, COLS], F32), ("junk3", [P, COLS], F32))
        gst = [gst0, gst1]
        y2 = yg

        banks = [ctx.enter_context(nc.psum_tensor(f"bank{b}", [P, COLS], F32)) for b in range(8)]
        SET_P, SET_Q = banks[:4], banks[4:]

        f_scr = nc.dram_tensor("f_scratch", [HEADS, S], F32, kind="Internal").ap()
        x1_scr = nc.dram_tensor("x1_scratch", [S, D], F32, kind="Internal").ap()

        raw_in = [sem(f"raw_in{i}") for i in range(RING)]
        hi_ready = sem("hi_ready")
        lo_ready = sem("lo_ready")
        lo_pool = sem("lo_pool")
        unit_used = sem("unit_used")
        ada_used = sem("ada_used")
        vec_in, c_in, bf_in, wf_in, gw_in = (sem(n) for n in ("vec_in", "c_in", "bf_in", "wf_in", "gw_in"))
        x_in = [sem(f"x_in{t}") for t in range(NT)]
        gst_in = [sem(f"gst_in{i}") for i in range(2)]
        gst_used = sem("gst_used")
        init_in = sem("init_in")
        acc_first = sem("acc_first")
        acc_read = sem("acc_read")
        mod_read = sem("mod_read")
        gain_in = sem("gain_in")
        gate_ready = sem("gate_ready")
        const_ready = sem("const_ready")
        vec_turned, vcol_ready = sem("vec_turned"), sem("vcol_ready")
        c_exp, dve_step, act_step, pool_step = (sem(n) for n in ("c_exp", "dve_step", "act_step", "pool_step"))
        lam_exp, kp_ready = sem("lam_exp"), sem("kp_ready")
        x_ssq, x_std, xdiag_ready, xt_done, xt_copied = (sem(n) for n in ("x_ssq", "x_std", "xdiag_ready", "xt_done", "xt_copied"))
        h_hi_ready, h_sum, h_lo_ready = (sem(n) for n in ("h_hi_ready", "h_sum", "h_lo_ready"))
        u_copied, conv_done, z_done, sig_done = (sem(n) for n in ("u_copied", "conv_done", "z_done", "sig_done"))
        decay_ready, m_ready, root_ready, ix_ready, bx_ready, scan_done, gelu_done, y_done, ssq_done = (
            sem(n) for n in ("decay_ready", "m_ready", "root_ready", "ix_ready", "bx_ready", "scan_done", "gelu_done",
                             "y_done", "ssq_done"))
        q_copied, k_copied, v_copied = sem("q_copied"), sem("k_copied"), sem("v_copied")
        wf_zero, wf_hi_ready, wf_lo_ready, f_done, f_read, f_exp = (
            sem(n) for n in ("wf_zero", "wf_hi_ready", "wf_lo_ready", "f_done", "f_read", "f_exp"))
        nf_ready, nf_stored, nfm_ready = sem("nf_ready"), sem("nf_stored"), sem("nfm_ready")
        nf_in = [sem(f"nf_in{i}") for i in range(2)]
        row_done, row_std, row_ready = sem("row_done"), sem("row_std"), sem("row_ready")
        yl_hi_ready, yl_lo_ready = sem("yl_hi_ready"), sem("yl_lo_ready")
        score_done, score_read, neg_max, exp_done, prob_ready, pt_done, pt_copied, pv_done = (
            sem(n) for n in ("score_done", "score_read", "neg_max", "exp_done", "prob_ready", "pt_done", "pt_copied", "pv_done"))
        ya_sq, ya_hi_ready, ya_lo_ready, att_ssq = (sem(n) for n in ("ya_sq", "ya_hi_ready", "ya_lo_ready", "att_ssq"))
        half_copied, y_sum, y_sq, y_gated = (sem(n) for n in ("half_copied", "y_sum", "y_sq", "y_gated"))
        mix_std, mix_sum, fin_sum = sem("mix_std"), sem("mix_sum"), sem("fin_sum")
        gw_zero = sem("gw_zero")
        xr_in = [sem(f"xr_in{t}") for t in range(NT)]
        x1_done, x1_ssq, x1_std, x1diag_ready, x1_stored = (sem(n) for n in ("x1_done", "x1_ssq", "x1_std", "x1diag_ready", "x1_stored"))
        x1t_done, h2_hi_ready, h2_lo_ready = (sem(n) for n in ("x1t_done", "h2_hi_ready", "h2_lo_ready"))
        relu_done, u_sq, u_hi_ready, u_lo_ready, y2_done = (sem(n) for n in ("relu_done", "u_sq", "u_hi_ready", "u_lo_ready", "y2_done"))
        x1r_in = sem("x1r_in")
        f_ssq, y2_gated, fin_std, out_ready, stored = (sem(n) for n in ("f_ssq", "y2_gated", "fin_std", "out_ready", "stored"))

        XS, XR, RL, RA, YS, YR, X1S, X1R_, FS, FR, NM, ES = 0, 4, 8, 12, 16, 32, 40, 44, 48, 64, 72, 80

        def col(base, i=0, n=1):
            return vcol[:, base + i:base + i + n]

        block = ctx.enter_context(nc.Block())

        SCORE_AT = {3: (banks[4], 0), 2: (banks[5], 0), 0: (banks[5], 3 * P), 1: (banks[6], 0)}
        LP_AT = [0, P, 3 * P, 6 * P]
        PT_PSUM = {0: (banks[4], 0), 1: (banks[5], 0), 3: (banks[5], 3 * P), 2: (banks[6], 0)}
        PT_AT = {0: 0, 1: 4 * P, 3: 7 * P, 2: 8 * P}
        GATE2_AFTER = (12, 18, 21, 26)

        @block.sync
        def _(sp):
            def slot_free(pos):
                if pos < RING:
                    return
                kind, n = stream[pos - RING]
                if kind == "ada":
                    sp.wait_ge(ada_used, n + 1)
                elif n < U_LAST and n % 2:
                    sp.wait_ge(lo_pool, n // 2 + 1)
                else:
                    sp.wait_ge(lo_ready, lo_count(n))

            def rows(w, r0, c0, tall=2, cols=COLS):
                return w[r0:r0 + tall * P, c0:c0 + cols].rearrange("(k p) n -> p k n", p=P)

            def source(n):
                if n < U_LAST:
                    return rows(w_in2, n // 2 * 2 * P, n % 2 * COLS)
                if n < U_PROJ:
                    return rows(w_in2, (n - U_LAST) * 8 * P, (CT - 1) * P, 8, P)
                if n < U_ATT:
                    g, v = divmod(n - U_PROJ, 8)
                    return rows(w_in2, v * 2 * P, D_LRU + g * COLS)
                if n < U_OUT:
                    g, v = divmod(n - U_ATT, 4)
                    return rows(w_out2, v * 2 * P, g * COLS)
                if n < U_MLP:
                    r, v = divmod(n - U_OUT, 4)
                    g, half = REST[r]
                    return rows(w_out2, half * D_LRU + v * 2 * P, g * COLS)
                return mlp_source(0, n - U_MLP)

            def mlp_source(ck, j):
                if j < 16:
                    g, v = divmod(j, 8)
                    return w_ff12[v * 2 * P:(v + 1) * 2 * P, bass.ds(ck * (FT * P) + g * COLS, COLS)].rearrange("(k p) n -> p k n", p=P)
                g, v = divmod(j - 16, 4)
                return w_ff22[bass.ds(ck * (FT * P) + v * 2 * P, 2 * P), g * COLS:(g + 1) * COLS].rearrange("(k p) n -> p k n", p=P)

            def load_init(m):
                if m:
                    sp.wait_ge(acc_first, m)
                parts = ((D + m * 256, 0, 256), (m * 256, 256, 256)) if m < 8 else ((ADA_COL[m - 8], 0, COLS),)
                for c0, at, width in parts:
                    sp.dma_start(acc_init[0:1, at:at + width], b_ada[0:1, c0:c0 + width]).then_inc(init_in, 16)

            def load(pos):
                slot, _ = place(pos)
                kind, n = stream[pos]
                if kind == "ada" and n % 8 == 0:
                    load_init(8 + n // 8)
                slot_free(pos)
                if kind == "ada":
                    cg, r = divmod(n, 8)
                    src = w_ada2[:, ADA_COL[cg]:ADA_COL[cg] + COLS].rearrange("(p k) n -> p k n", p=P)[:, 2 * r:2 * r + 2]
                else:
                    src = source(n)
                dst = raw[:, slot].rearrange("p (k n) -> p k n", k=src.shape[1])
                sp.dma_start(dst, src).then_inc(raw_in[slot], 16)

            def start_half(j, half):
                i = 2 * j + half
                if half == 0:
                    load_init(j)
                if i >= 2:
                    sp.wait_ge(gst_used, i - 1)
                for part, base in enumerate((D, 0)):
                    src = w_ada2[:, base + j * 256:base + (j + 1) * 256].rearrange("(p k) n -> p k n", p=P)
                    sp.dma_start(gst[half][:, :, part, :], src[:, 8 * half:8 * half + 8]).then_inc(gst_in[half], 16)

            sp.wait_ge(const_ready, 4)
            start_half(0, 0)
            for t in range(NT):
                sp.dma_start(x_tok[:, t], x2[t * P:(t + 1) * P, :]).then_inc(x_in[t], 16)
            for j in range(8):
                if j:
                    start_half(j, 0)
                start_half(j, 1)
                for n in (2 * j, 2 * j + 1):
                    load(main_pos[n])
            for pos in range(main_pos[U_LAST], POS_LOOP):
                load(pos)

            def chunk(ck):
                for j in range(PER_CHUNK):
                    slot, _ = chunk_raw(1, j)
                    sp.wait_ge(lo_ready, ck * PER_CHUNK + (U_MLP + j - RING - 7))
                    sp.dma_start(raw[:, slot].rearrange("p (k n) -> p k n", k=2), mlp_source(ck, j)).then_inc(raw_in[slot], 16)

            with sp.Fori(1, CHUNKS - 1) as ck:
                chunk(ck)
            chunk(CHUNKS - 1)
            for t in range(NT):
                sp.wait_ge(out_ready, t + 1)
                sp.dma_start(out2[t * P:(t + 1) * P, :], x1r[:, t]).then_inc(stored, 16)
            sp.wait_ge(stored, 16 * NT)

        @block.tensor
        def _(pe):
            def unit_ready(n):
                if n < U_LAST and n % 2:
                    pe.wait_ge(lo_pool, n // 2 + 1)
                else:
                    pe.wait_ge(lo_ready, lo_count(n))

            def w_tile(slot, k, width=COLS):
                return (w_hi[:, slot, k * width:(k + 1) * width], w_lo[:, slot, k * width:(k + 1) * width])

            def feature_major(bank_of, w, act_hi, act_lo, kt, n_kt, blocks=range(4)):
                hi, lo = w
                for m in blocks:
                    b, cols = bank_of[m], slice(m * P, (m + 1) * P)
                    pe.matmul(b[:, :], lo[:, cols], act_hi[:, kt, :], start=(kt == 0), stop=False)
                    pe.matmul(b[:, :], hi[:, cols], act_lo[:, kt, :], start=False, stop=False)
                    last = pe.matmul(b[:, :], hi[:, cols], act_hi[:, kt, :], start=False, stop=(kt == n_kt - 1))
                return last

            def token_major(bank_of, w, act_hi, act_lo, kt, n_kt):
                hi, lo = w
                for t in range(NT):
                    b, tok = bank_of[t], slice(t * P, (t + 1) * P)
                    pe.matmul(b[:, :], act_lo[:, kt, tok], hi, start=(kt == 0), stop=False)
                    pe.matmul(b[:, :], act_hi[:, kt, tok], lo, start=False, stop=False)
                    last = pe.matmul(b[:, :], act_hi[:, kt, tok], hi, start=False, stop=(kt == n_kt - 1))
                return last

            def sums_ready(m):
                if m < 8:
                    pe.wait_ge(gst_used, 2 * (m + 1))
                else:
                    pe.wait_ge(ada_used, 8 * (m - 7))

            def column_job(m, bank):
                sums_ready(m)
                for b in range(4):
                    last = pe.matmul(bank[:, b:b + 1], acc[:, m % 2, b * P:(b + 1) * P], ones[:, 0:1], start=True, stop=True)
                last.then_inc(acc_read, 1)

            def row_job(m, bank):
                sums_ready(m)
                pe.matmul(bank[:, :], ones[:, :], acc[:, m % 2, :], start=True, stop=True).then_inc(acc_read, 1)

            def stats_job(bank):
                for t in range(NT):
                    last = pe.matmul(bank[:, t:t + 1], ssq[:, t * P:(t + 1) * P], ones[:, 0:1], start=True, stop=True)
                last.then_inc(row_done, 1)

            pe.wait_ge(const_ready, 2)
            pe.wait_ge(vec_in, 16 * 9)
            pe.transpose(banks[7][:, 0:112], vrow[0:112, :], ident[0:112, 0:112]).then_inc(vec_turned, 1)
            pe.wait_ge(xdiag_ready, NT)
            for kt in range(KT):
                if kt >= 4:
                    pe.wait_ge(xt_copied, kt - 3)
                for t in range(NT):
                    last = pe.matmul(banks[kt % 4][:, t * P:(t + 1) * P], x_tok[:, t, kt * P:(kt + 1) * P], xdiag[:, t, :],
                                     start=True, stop=True)
                last.then_inc(xt_done, 1)

            for j in range(8):
                pe.wait_ge(mod_read, j) if j else pe.wait_ge(vcol_ready, 1)
                column_job(j, banks[7])
                if j == 0:
                    pe.wait_ge(xt_copied, KT)
                for n, group, blocks in ((2 * j, SET_P, range(4)), (2 * j + 1, SET_Q, range(3))):
                    unit_ready(n)
                    for k in range(2):
                        pe.wait_ge(h_lo_ready, 2 * j + k + 1)
                        last = feature_major(group, w_tile(n % RING, k), h_hi, h_lo, 2 * j + k, KT, blocks)
                    last.then_inc(unit_used, 1)
            pe.wait_ge(mod_read, 8)
            for n in (U_LAST, U_LAST + 1):
                unit_ready(n)
                for k in range(8):
                    last = feature_major([banks[7]], w_tile(n % RING, k, P), h_hi, h_lo, 8 * (n - U_LAST) + k, KT, range(1))
                last.then_inc(unit_used, 1)

            def gates(ch):
                pe.wait_ge(conv_done, ch + 1)
                if ch < 2:
                    pe.wait_ge(u_copied, 6 + 2 * ch)
                else:
                    pe.wait_ge(sig_done, 2 * (ch - 1))
                b = 4 + 2 * (ch % 2)
                pe.matmul(banks[b][:, :], wrg[:, ch, :], hs[:, ch, :], start=True, stop=True)
                pe.matmul(banks[b + 1][:, :], wig[:, ch, :], hs[:, ch, :], start=True, stop=True).then_inc(z_done, 1)

            GATES_AFTER = {U_PROJ: [0], U_PROJ + 1: [1], U_PROJ + 2: [2], U_PROJ + 3: [3], U_PROJ + 5: [4, 5], U_PROJ + 7: [6, 7]}
            pe.wait_ge(gw_in, 64)
            for gi in range(8):
                bank_of = (SET_P, SET_Q)[gi % 2]
                other = (SET_Q, SET_P)[gi % 2][0]
                if gi >= 2:
                    pe.wait_ge(mod_read, 8 + gi - 1)
                if gi == 0:
                    pe.wait_ge(u_copied, 4)
                elif gi == 1:
                    pe.wait_ge(sig_done, 16)
                elif gi in (2, 3):
                    pe.wait_ge(gelu_done, 4 * (gi - 1))
                elif gi in (4, 5):
                    pe.wait_ge(q_copied, 4 * (gi - 3))
                else:
                    bank_of = (SET_Q, SET_P)[gi % 2]
                    other = (SET_P, SET_Q)[gi % 2][1]
                    if gi == 6:
                        pe.wait_ge(k_copied, 4)
                        pe.wait_ge(wf_lo_ready, 1)
                        for kt in range(KT):
                            last = feature_major([banks[0]], (wf_hi[:, kt, :], wf_lo[:, kt, :]), h_hi, h_lo, kt, KT, range(1))
                        last.then_inc(f_done, 1)
                        pe.wait_ge(k_copied, 8)
                    else:
                        pe.wait_ge(f_read, 1)
                        pe.wait_ge(row_std, 1)
                for v in range(8):
                    n = U_PROJ + 8 * gi + v
                    unit_ready(n)
                    for k in range(2):
                        w = w_tile(n % RING, k)
                        if gi < 6:
                            last = feature_major(bank_of, w, h_hi, h_lo, 2 * v + k, KT)
                        else:
                            last = token_major(bank_of, w, h_hi, h_lo, 2 * v + k, KT)
                    last.then_inc(unit_used, 1)
                    for ch in GATES_AFTER.get(n, []):
                        gates(ch)
                    if gi and v == COLUMNS_AT[gi]:
                        for s, count in {1: [(gelu_done, 4)], 2: [(gelu_done, 8)], 3: [(q_copied, 4)], 4: [(q_copied, 8)],
                                         5: [(k_copied, 4)], 6: [(k_copied, 4)], 7: [(v_copied, 4)]}[gi]:
                            pe.wait_ge(s, count)
                        column_job(8 + gi - 1, other)
                    if gi == 6 and v == 6:
                        pe.wait_ge(ssq_done, CT)
                        stats_job(banks[2])
                    if gi == 7 and v == 6:
                        pe.wait_ge(mod_read, 8 + 7)
                        column_job(8 + 7, banks[6])

            def scores(h):
                if h == 0:
                    pe.wait_ge(q_copied, HEADS)
                    pe.wait_ge(k_copied, HEADS)
                    pe.wait_ge(v_copied, 4)
                    pe.wait_ge(mod_read, 8 + 8)
                else:
                    pe.wait_ge(pt_copied, 3 * h)
                for i in (1, 0, 2, 3):
                    n_keys = (i + 1) * P
                    b, c0 = SCORE_AT[i]
                    last = pe.matmul(b[:, c0:c0 + n_keys], qT[:, h, i * P:(i + 1) * P], kT[:, h, 0:n_keys], start=True, stop=True)
                    if i != 0:
                        last.then_inc(score_done, 1)

            def turn_probs(h):
                pe.wait_ge(prob_ready, 4 * (h + 1))
                for j in (2, 1, 3, 0):
                    b, c0 = PT_PSUM[j]
                    for i in range(j, NT):
                        last = pe.transpose(b[:, c0 + (i - j) * P:c0 + (i - j + 1) * P],
                                            LP[:, LP_AT[i] + j * P:LP_AT[i] + (j + 1) * P], ident[:, :])
                    if j != 1:
                        last.then_inc(pt_done, 1)

            def weigh_values(h):
                pe.wait_ge(pt_copied, 3 * (h + 1))
                if h == 0:
                    pe.wait_ge(v_copied, 8)
                else:
                    pe.wait_ge(ya_lo_ready, h)
                for j in range(NT):
                    last = pe.matmul(banks[7][:, j * P:S], vv[:, j, h * P:(h + 1) * P], PT[:, PT_AT[j]:PT_AT[j] + S - j * P],
                                     start=(j == 0), stop=(j == NT - 1))
                last.then_inc(pv_done, 1)

            def beside_attention(h, k):
                g, v = divmod(h, 4)
                n = U_ATT + h
                if k == 0:
                    unit_ready(n)
                    if v == 0:
                        pe.wait_ge(v_copied, 8) if g == 0 else pe.wait_ge(half_copied, 4)
                pe.wait_ge(yl_lo_ready, 2 * v + k + 1)
                last = token_major(SET_P, w_tile(n % RING, k), yl_hi, yl_lo, 2 * v + k, CT)
                if k:
                    last.then_inc(unit_used, 1)

            scores(0)
            for h in range(HEADS):
                beside_attention(h, 0)
                turn_probs(h)
                beside_attention(h, 1)
                if h < HEADS - 1:
                    scores(h + 1)
                weigh_values(h)

            for r, (g, half) in enumerate(REST):
                bank_of = (SET_P, SET_Q)[r % 2]
                if r == 0:
                    pe.wait_ge(half_copied, 8)
                elif r == 1:
                    pe.wait_ge(ya_lo_ready, HEADS)
                    pe.wait_ge(row_std, 2)
                    pe.wait_ge(gate_ready, 1)
                elif r == 2:
                    pe.wait_ge(half_copied, 12)
                else:
                    pe.wait_ge(y_sum, 4 * (r - 2))
                    pe.wait_ge(gate_ready, r - 1)
                for v in range(4):
                    n = U_OUT + 4 * r + v
                    unit_ready(n)
                    for k in range(2):
                        last = token_major(bank_of, w_tile(n % RING, k), (yl_hi, ya_hi)[half], (yl_lo, ya_lo)[half], 2 * v + k, CT)
                    last.then_inc(unit_used, 1)
                    if r == 0 and v == 1:
                        pe.wait_ge(att_ssq, HEADS)
                        pe.wait_ge(pt_copied, 3 * HEADS)
                        stats_job(banks[4])
                    if v == 2 and r in (0, 2, 3, 4):
                        if r:
                            pe.wait_ge(y_sum, 4 * (r - 1))
                        row_job(16 + max(r - 1, 0), banks[5] if r == 0 else (SET_Q, SET_P)[r % 2][0])

            def turn_x1(kt):
                pe.wait_ge(x1diag_ready, NT)
                if kt >= 4:
                    pe.wait_ge(h2_lo_ready, kt - 3)
                else:
                    pe.wait_ge(y_sum, 16)
                for t in range(NT):
                    last = pe.matmul(SET_Q[kt % 4][:, t * P:(t + 1) * P], yg[:, t, kt * P:(kt + 1) * P], x1diag[:, t, :],
                                     start=True, stop=True)
                last.then_inc(x1t_done, 1)

            def chunk(ck, first=False):
                n_of = lambda j: U_MLP + j
                slot_of = lambda j: (U_MLP + j) % RING
                if first:
                    for kt in range(4):
                        turn_x1(kt)
                    pe.wait_ge(half_copied, 16)
                else:
                    pe.wait_ge(y2_done, ck * 16 - 4)
                for j in range(PER_CHUNK):
                    if j == 8:
                        pe.wait_ge(h2_lo_ready, KT) if first else pe.wait_ge(y2_done, ck * 16)
                    elif j == 16:
                        pe.wait_ge(relu_done, ck * 8 + 4)
                        if first:
                            pe.wait_ge(gate_ready, 5)
                    elif j == 20:
                        pe.wait_ge(relu_done, ck * 8 + 8)
                        if first:
                            pe.wait_ge(gate_ready, 6)
                    elif j == 24:
                        pe.wait_ge(y2_done, ck * 16 + 4)
                        if first:
                            pe.wait_ge(gate_ready, 7)
                    elif j == 28:
                        pe.wait_ge(y2_done, ck * 16 + 8)
                        if first:
                            pe.wait_ge(gate_ready, 8)
                    pe.wait_ge(lo_ready, ck * PER_CHUNK + (n_of(j) - 7))
                    for k in range(2):
                        w = w_tile(slot_of(j), k)
                        if j < 16:
                            kt = 2 * (j % 8) + k
                            if first and j < 8:
                                pe.wait_ge(h2_lo_ready, kt + 1)
                            last = feature_major((SET_P, SET_Q)[j // 8], w, h_hi, h_lo, kt, KT)
                        else:
                            g, v = divmod(j - 16, 4)
                            pe.wait_ge(u_lo_ready, ck * 8 + (2 * v + k + 1))
                            last = token_major((SET_P, SET_Q)[g % 2], w, u_hi, u_lo, 2 * v + k, FT)
                    last.then_inc(unit_used, 1)
                    if first and j < 6:
                        turn_x1(2 * j + 4)
                        turn_x1(2 * j + 5)
                    if first and j in GATE2_AFTER:
                        q = GATE2_AFTER.index(j)
                        if q < 2:
                            pe.wait_ge(relu_done, 4 * (q + 1))
                        else:
                            pe.wait_ge(y2_done, 4 * (q - 1))
                        row_job(20 + q, banks[4 * (q % 2)])

            chunk(0, first=True)
            with pe.Fori(1, CHUNKS - 1) as ck:
                chunk(ck)
            chunk(CHUNKS - 1)

        @block.scalar
        def _(act):
            steps = [0]

            def step(ins):
                ins.then_inc(act_step, 1)
                steps[0] += 1
                act.wait_ge(act_step, steps[0])

            def hi_part(n):
                slot, count, s = unit(n)
                act.wait_ge(raw_in[slot], count)
                if n >= RING:
                    act.wait_ge(unit_used, n - RING + 1)
                act.activation(w_hi[:, s], raw[:, slot], ACT.Copy).then_inc(hi_ready, 1)

            act.dma_start(cc[:, 0, :], c.rearrange("b (p k) -> (b p) k", p=P)).then_inc(c_in, 16)
            for row, v, tall in ((G_PRE_MIX, g_pre_mix, KT), (G_PRE_MLP, g_pre_mlp, KT), (CONVB, conv_b, CT), (B_RG, b_rg, CT),
                                 (B_IG, b_ig, CT), (LAMBDA, lru_lambda, CT), (G_LRU, g_lru_out, CT), (G_ATT, g_att_out, CT)):
                act.dma_start(vrow[row:row + tall, :], v.rearrange("l (r n) -> (l r) n", n=P)).then_inc(vec_in, 16)
            act.dma_start(vrow[CONVW:CONVW + CW * CT, :], conv_w.rearrange("l w (r n) -> (l w r) n", n=P)).then_inc(vec_in, 16)
            act.dma_start(bf[:, :], b_forget.rearrange("l h -> h l")).then_inc(bf_in, 16)
            act.dma_start(wf_raw[:, :, :], w_in2[:, 2 * D_LRU + 3 * D_ATT:].rearrange("(k p) n -> p k n", p=P)).then_inc(wf_in, 16)

            act.wait_ge(c_in, 16)
            act.activation(cc[:, 1, :], cc[:, 0, :], ACT.Exp, scale=-1.0).then_inc(c_exp, 1)
            act.wait_ge(vec_turned, 1)
            act.activation(vcol[:, :], banks[7][:, 0:112], ACT.Copy).then_inc(vcol_ready, 1)
            act.wait_ge(vcol_ready, 1)
            step(act.activation(lam[:, 0, :], col(LAMBDA, 0, CT), ACT.Abs))
            act.activation(lam[:, 1, :], lam[:, 0, :], ACT.Exp, scale=-1.0).then_inc(lam_exp, 1)
            for t in range(NT):
                act.wait_ge(x_in[t], 16)
                if t:
                    act.wait_ge(x_ssq, t)
                act.activation(junk[:, :], x_tok[:, t], ACT.Square, accum_out=stat[:, XS + t:XS + t + 1]).then_inc(x_ssq, 1)
            act.wait_ge(x_ssq, NT)
            act.activation(stat[:, XR:XR + NT], stat[:, XS:XS + NT], ACT.Sqrt, bias=eps[:, :], scale=1.0 / D).then_inc(x_std, 1)
            for kt in range(KT):
                act.wait_ge(xt_done, kt + 1)
                act.activation(xnT[:, kt, :], banks[kt % 4][:, :], ACT.Copy).then_inc(xt_copied, 1)

            act.wait_ge(gw_zero, 2)
            for w, dst in ((w_rg, wrg), (w_ig, wig)):
                for b in range(2):
                    act.dma_start(dst[b * LB:(b + 1) * LB, :, b * LB:(b + 1) * LB],
                                  w[0, b:2 * CT:2].rearrange("n i j -> i n j")).then_inc(gw_in, 16)

            act.wait_ge(xt_copied, KT)
            for j in range(8):
                act.wait_ge(mod_read, j + 1)
                for kt in (2 * j, 2 * j + 1):
                    act.activation(h_hi[:, kt, :], xnT[:, kt, :], ACT.Identity, bias=S1[:, kt:kt + 1],
                                   scale=A1[:, kt:kt + 1]).then_inc(h_hi_ready, 1)
                hi_part(2 * j)
                hi_part(2 * j + 1)

            def copy_u(ch):
                act.activation(ut[:, ch, :], banks[ch][:, :], ACT.Copy).then_inc(u_copied, 1)

            def sigmoids(ch):
                act.wait_ge(z_done, ch + 1)
                b = 4 + 2 * (ch % 2)
                act.activation(rg[:, ch, :], banks[b][:, :], ACT.Sigmoid, bias=col(B_RG, ch)).then_inc(sig_done, 1)
                act.activation(ig[:, ch, :], banks[b + 1][:, :], ACT.Sigmoid, bias=col(B_IG, ch)).then_inc(sig_done, 1)

            def decay(ch):
                act.wait_ge(kp_ready, 1)
                act.wait_ge(sig_done, 2 * ch + 1)
                act.activation(ut[:, ch, :], rg[:, ch, :], ACT.Tanh, scale=lam[:, 6, ch:ch + 1])
                step(act.activation(rg[:, ch, :], rg[:, ch, :], ACT.Exp, scale=lam[:, 7, ch:ch + 1]))
                if ch >= 2:
                    act.wait_ge(m_ready, ch - 1)
                act.activation(a_sq[:, ch % 2, :], rg[:, ch, :], ACT.Square).then_inc(decay_ready, 1)

            def root(ch):
                act.wait_ge(m_ready, ch + 1)
                act.activation(ut[:, ch, :], ut[:, ch, :], ACT.Sqrt).then_inc(root_ready, 1)

            def gelu(ch):
                act.wait_ge(unit_used, U_PROJ + (8 if ch < 4 else 16))
                act.wait_ge(bx_ready, ch + 1)
                act.activation(ut[:, ch, :], banks[ch][:, :], ACT.Gelu_apprx_tanh).then_inc(gelu_done, 1)

            for n in range(U_LAST, U_ATT + LAG):
                hi_part(n)
                done = n - LAG + 1
                if done == U_LAST:
                    act.wait_ge(unit_used, U_LAST)
                    for ch in range(CT - 1):
                        copy_u(ch)
                if done == U_PROJ:
                    act.wait_ge(unit_used, U_PROJ)
                    copy_u(CT - 1)
                e = n - U_PROJ
                for ch in {3: [0], 4: [1], 5: [2], 6: [3], 8: [4, 5], 10: [6, 7]}.get(e, []):
                    sigmoids(ch)
                for ch in {7: [0, 1, 2, 3], 11: [4, 5], 12: [6, 7]}.get(e, []):
                    decay(ch)
                if e == 13:
                    for ch in range(CT):
                        root(ch)
                if e == 14:
                    for ch in range(4):
                        gelu(ch)
                if e == 18:
                    for ch in range(4, 8):
                        gelu(ch)
                if e == 30:
                    act.wait_ge(wf_in, 16)
                    act.wait_ge(wf_zero, 2)
                    act.activation(wf_hi[:, :, 0:HEADS], wf_raw[:, :, :], ACT.Copy).then_inc(wf_hi_ready, 1)
                for gi, dst, done_sem in ((2, qT, q_copied), (3, qT, q_copied), (4, kT, k_copied), (5, kT, k_copied)):
                    if done == U_PROJ + 8 * (gi + 1):
                        act.wait_ge(unit_used, done)
                        if gi == 2:
                            act.wait_ge(scan_done, CT)
                        if gi == 4:
                            act.wait_ge(scan_done, CT)
                        for m in range(4):
                            act.activation(dst[:, 4 * (gi % 2) + m, :], banks[4 * (gi % 2) + m][:, :], ACT.Copy,
                                           scale=DH ** -0.5 if dst is qT else 1.0).then_inc(done_sem, 1)
                if e == 6 * 8 + 3:
                    act.wait_ge(f_done, 1)
                    act.wait_ge(bf_in, 16)
                    act.wait_ge(ssq_done, CT)
                    act.activation(ut[0:HEADS, 0, :], banks[0][0:HEADS, :], ACT.Identity, bias=bf[:, :]).then_inc(f_read, 1)
                    act.wait_ge(f_read, 1)
                    step(act.activation(ut[0:HEADS, 1, :], ut[0:HEADS, 0, :], ACT.Abs))
                    act.activation(ut[0:HEADS, 2, :], ut[0:HEADS, 1, :], ACT.Exp, scale=-1.0).then_inc(f_exp, 1)
                if e == 7 * 8 + 1:
                    act.wait_ge(row_done, 1)
                    act.activation(stat[:, RL:RL + NT], banks[2][:, 0:NT], ACT.Sqrt, bias=eps[:, :], scale=1.0 / D_LRU).then_inc(row_std, 1)
                for gi in (6, 7):
                    if done == U_PROJ + 8 * (gi + 1):
                        act.wait_ge(unit_used, done)
                        act.wait_ge(nf_stored, 16)
                        for t in range(NT):
                            act.activation(vv[:, t, (gi - 6) * COLS:(gi - 5) * COLS], banks[(4, 0)[gi - 6] + t][:, :],
                                           ACT.Copy).then_inc(v_copied, 1)

            for ch in range(CT):
                act.activation(yl_hi[:, ch, :], hs[:, ch, :], ACT.Copy, scale=col(G_LRU, ch)).then_inc(yl_hi_ready, 1)

            def exps(h):
                for e, i in enumerate((1, 0, 2, 3)):
                    act.wait_ge(neg_max, 4 * h + e + 1)
                    n_keys = (i + 1) * P
                    act.activation(LP[:, LP_AT[i]:LP_AT[i] + n_keys], LP[:, LP_AT[i]:LP_AT[i] + n_keys], ACT.Exp,
                                   bias=stat[:, NM + i:NM + i + 1], accum_out=stat[:, ES + i:ES + i + 1]).then_inc(exp_done, 1)

            def copy_pt(h):
                if h:
                    act.wait_ge(pv_done, h)
                for e, (b, c0, width, dst) in enumerate(((banks[6], 0, 2 * P, PT_AT[2]), (banks[5], 0, 4 * P, PT_AT[1]),
                                                         (banks[4], 0, 4 * P, PT_AT[0]))):
                    act.wait_ge(pt_done, 3 * h + e + 1)
                    act.activation(PT[:, dst:dst + width], b[:, c0:c0 + width], ACT.Copy).then_inc(pt_copied, 1)

            def head_out(h):
                act.wait_ge(pv_done, h + 1)
                if h:
                    act.wait_ge(att_ssq, h)
                act.activation(g_row[:, :], banks[7][:, :], ACT.Square).then_inc(ya_sq, 1)
                act.activation(ya_hi[:, h, :], banks[7][:, :], ACT.Copy, scale=col(G_ATT, h)).then_inc(ya_hi_ready, 1)

            def copy_half(bank_of, dst):
                for t in range(NT):
                    act.activation(dst(t), bank_of[t][:, :], ACT.Copy, scale=stat[:, RL + t:RL + t + 1]).then_inc(half_copied, 1)

            act.wait_ge(row_ready, 1)
            for h in range(HEADS):
                exps(h)
                if h:
                    head_out(h - 1)
                hi_part(U_ATT + LAG + h)
                copy_pt(h)
                if h % 4 == 3:
                    act.wait_ge(unit_used, U_ATT + h + 1)
                    if h == 3:
                        act.wait_ge(yl_lo_ready, CT)
                    copy_half(SET_P, lambda t: yacc[:, t, h // 4, :])
            head_out(HEADS - 1)

            def mix_evacuation(r):
                g, half = REST[r]
                cols = slice(g * COLS, (g + 1) * COLS)
                if half == 0:
                    act.wait_ge(unit_used, U_OUT + 4 * r + 4)
                    copy_half(SET_P, lambda t: yg[:, t, cols])
                else:
                    e = 4 * [1, 2, 3, 5].index(r)
                    for t in range(NT):
                        act.wait_ge(y_sum, e + t + 1)
                        if e + t:
                            act.wait_ge(y_sq, e + t)
                        act.activation(junk2[:, 0:COLS], yg[:, t, cols], ACT.Square,
                                       accum_out=stat[:, YS + 4 * t + g:YS + 4 * t + g + 1]).then_inc(y_sq, 1)

            for n in range(U_OUT + LAG, U_MLP + LAG):
                hi_part(n)
                done = n - LAG + 1 - U_OUT
                if done == 3:
                    act.wait_ge(row_done, 2)
                    act.activation(stat[:, RA:RA + NT], banks[4][:, 0:NT], ACT.Sqrt, bias=eps[:, :], scale=1.0 / D_ATT).then_inc(row_std, 1)
                if done and done % 4 == 0:
                    mix_evacuation(done // 4 - 1)

            act.wait_ge(mix_sum, 1)
            act.activation(stat[:, YR:YR + NT], stat[:, YR:YR + NT], ACT.Sqrt, bias=eps[:, :], scale=1.0 / D).then_inc(mix_std, 1)
            for t in range(NT):
                act.wait_ge(x1_done, t + 1)
                act.wait_ge(x1_ssq, t) if t else act.wait_ge(y_sq, 16)
                act.activation(junk2[:, :], yg[:, t, :], ACT.Square, accum_out=stat[:, X1S + t:X1S + t + 1]).then_inc(x1_ssq, 1)
                act.wait_ge(x1_ssq, t + 1)
                act.activation(stat[:, X1S + t:X1S + t + 1], stat[:, X1S + t:X1S + t + 1], ACT.Sqrt, bias=eps[:, :],
                               scale=1.0 / D).then_inc(x1_std, 1)

            def modulate(kt):
                act.wait_ge(x1t_done, kt + 1)
                act.activation(h_hi[:, kt, :], SET_Q[kt % 4][:, :], ACT.Identity, bias=S2[:, kt:kt + 1],
                               scale=A2[:, kt:kt + 1]).then_inc(h2_hi_ready, 1)

            def hidden(ck, g):
                for m in range(4):
                    e = 4 * g + m
                    act.wait_ge(unit_used, ck * PER_CHUNK + (U_MLP + 8 * (g + 1)))
                    if e >= 2 or not (isinstance(ck, int) and ck == 0):
                        act.wait_ge(u_sq, ck * 8 + (e - 1))
                    act.activation(rt[:, m % 2, :], (SET_P, SET_Q)[g][m][:, :], ACT.Relu).then_inc(relu_done, 1)
                    act.wait_ge(relu_done, ck * 8 + (e + 1))
                    act.activation(u_hi[:, e, :], rt[:, m % 2, :], ACT.Square).then_inc(u_hi_ready, 1)

            def hi_of_chunk(ck, j):
                slot, count = chunk_raw(ck, j)
                act.wait_ge(raw_in[slot], count)
                act.wait_ge(unit_used, ck * PER_CHUNK + (U_MLP + j - RING + 1))
                act.activation(w_hi[:, (U_MLP + j) % RING], raw[:, slot], ACT.Copy).then_inc(hi_ready, 1)

            def chunk(ck, j0=0, last=False):
                for j in range(j0, PER_CHUNK):
                    hi_of_chunk(ck, j)
                    if j == 7 + LAG:
                        hidden(ck, 0)
                    if j == 15 + LAG:
                        hidden(ck, 1)
                    if last and j in (19 + LAG, 23 + LAG, 27 + LAG):
                        final_squares((j - 19 - LAG) // 4)

            def final_squares(g):
                for t in range(NT):
                    act.wait_ge(y2_done, 16 * (CHUNKS - 1) + 4 * g + t + 1)
                    if g or t:
                        act.wait_ge(f_ssq, 4 * g + t)
                    act.activation(junk3[:, :], y2[:, t, g * COLS:(g + 1) * COLS], ACT.Square,
                                   accum_out=stat[:, FS + 4 * t + g:FS + 4 * t + g + 1]).then_inc(f_ssq, 1)

            for kt in range(KT):
                modulate(kt)
                if kt >= 5 and kt % 2:
                    hi_of_chunk(0, LAG + (kt - 5) // 2)
            chunk(0, LAG + 6)
            with act.Fori(1, CHUNKS - 1) as ck:
                chunk(ck)
            chunk(CHUNKS - 1, last=True)
            final_squares(3)
            act.wait_ge(fin_sum, 1)
            act.activation(stat[:, FR:FR + NT], stat[:, FR:FR + NT], ACT.Sqrt, bias=eps[:, :], scale=1.0 / D).then_inc(fin_std, 1)

        @block.vector
        def _(dve):
            steps = [0]

            def step(ins):
                ins.then_inc(dve_step, 1)
                steps[0] += 1
                dve.wait_ge(dve_step, steps[0])

            def lo_part(n):
                slot, _, s = unit(n)
                dve.wait_ge(hi_ready, n + 1)
                dve.tensor_tensor(w_lo[:, s], raw[:, slot], w_hi[:, s].bitcast(F32), ALU.subtract).then_inc(lo_ready, 1)

            def log1p_part(e, d, s, s2, q):
                step(dve.tensor_scalar(d, e, 2.0, None, ALU.add))
                step(dve.reciprocal(d, d))
                step(dve.tensor_tensor(s, e, d, ALU.mult))
                step(dve.tensor_tensor(s2, s, s, ALU.mult))
                step(dve.tensor_scalar(q, s2, 1.0 / 17, None, ALU.mult))
                for k in range(7, 0, -1):
                    step(dve.scalar_tensor_tensor(q, q, 1.0 / (2 * k + 1), s2, ALU.add, ALU.mult))
                step(dve.scalar_tensor_tensor(q, q, 1.0, s, ALU.add, ALU.mult))

            dve.wait_ge(c_exp, 1)
            step(dve.tensor_scalar(cc[:, 1, :], cc[:, 1, :], 1.0, None, ALU.add))
            step(dve.reciprocal(cc[:, 1, :], cc[:, 1, :]))
            step(dve.tensor_tensor(cc[:, 2, :], cc[:, 0, :], cc[:, 1, :], ALU.mult))

            def weigh_rows(m, k0, rows, used, count):
                a = acc[:, m % 2, :]
                for r, row in enumerate(rows):
                    k = k0 + r
                    if k == 0:
                        dve.wait_ge(init_in, 32 * (m + 1) if m < 8 else 16 * (m + 9))
                        if m >= 2:
                            dve.wait_ge(acc_read, m - 1)
                    ins = dve.scalar_tensor_tensor(a, row, cc[:, 2, k:k + 1], a if k else acc_init[:, :], ALU.mult, ALU.add)
                    if k == 0:
                        ins.then_inc(acc_first, 1)
                        dve.wait_ge(acc_first, m + 1)
                    elif r == len(rows) - 1:
                        ins.then_inc(used, 1)
                        dve.wait_ge(used, count)
                    else:
                        step(ins)

            def start_sums(j, half):
                dve.wait_ge(gst_in[half], 32 * (j + 1))
                weigh_rows(j, 8 * half, [gst[half][:, r].rearrange("p a b -> p (a b)") for r in range(8)],
                           gst_used, 2 * j + half + 1)

            def ada_unit(a):
                cg, r = divmod(a, 8)
                slot, count = place(ada_pos[a])
                dve.wait_ge(raw_in[slot], count)
                weigh_rows(8 + cg, 2 * r, [raw[:, slot, 0:COLS], raw[:, slot, COLS:]], ada_used, a + 1)

            def take_start(j):
                dve.wait_ge(acc_read, j + 1)
                step(dve.scalar_tensor_tensor(A1[:, 2 * j:2 * j + 2], banks[7][:, 0:2], 1.0, col(G_PRE_MIX, 2 * j, 2), ALU.add, ALU.mult))
                dve.tensor_copy(S1[:, 2 * j:2 * j + 2], banks[7][:, 2:4]).then_inc(mod_read, 1)

            def take_columns(cg, bank):
                dve.wait_ge(acc_read, 8 + cg + 1)
                if cg < 4:
                    dve.scalar_tensor_tensor(A2[:, 4 * cg:4 * cg + 4], bank[:, 0:4], 1.0, col(G_PRE_MLP, 4 * cg, 4),
                                             ALU.add, ALU.mult).then_inc(mod_read, 1)
                else:
                    dve.tensor_copy(S2[:, 4 * cg - 16:4 * cg - 12], bank[:, 0:4]).then_inc(mod_read, 1)

            def take_gate(q, bank):
                dve.wait_ge(acc_read, 17 + q)
                dve.wait_ge(gain_in, 16 * (q + 1))
                dst = (G1, G2)[q // 4][:, q % 4 * COLS:(q % 4 + 1) * COLS]
                dve.tensor_tensor(dst, bank[:, :], g_row[:, :], ALU.mult).then_inc(gate_ready, 1)

            def h_low(kt):
                dve.wait_ge(h_sum, kt + 1)
                dve.tensor_tensor(h_lo[:, kt, :], xnT[:, kt, :], h_hi[:, kt, :].bitcast(F32), ALU.subtract).then_inc(h_lo_ready, 1)

            dve.wait_ge(const_ready, 4)
            start_sums(0, 0)
            start_sums(0, 1)
            dve.wait_ge(lam_exp, 1)
            log1p_part(lam[:, 1, :], lam[:, 2, :], lam[:, 3, :], lam[:, 4, :], lam[:, 5, :])
            step(dve.tensor_scalar(lam[:, 2, :], col(LAMBDA, 0, CT), -1.0, 0.0, ALU.mult, ALU.max))
            step(dve.scalar_tensor_tensor(lam[:, 3, :], lam[:, 5, :], 2.0, lam[:, 2, :], ALU.mult, ALU.add))
            step(dve.tensor_scalar(lam[:, 6, :], lam[:, 3, :], LRU_C, None, ALU.mult))
            dve.tensor_scalar(lam[:, 7, :], lam[:, 3, :], -LRU_C, None, ALU.mult).then_inc(kp_ready, 1)
            dve.wait_ge(x_std, 1)
            step(dve.reciprocal(stat[:, XR:XR + NT], stat[:, XR:XR + NT]))
            for t in range(NT):
                dve.tensor_scalar(xdiag[:, t, :], ident[:, :], stat[:, XR + t:XR + t + 1], None, ALU.mult).then_inc(xdiag_ready, 1)
            for j in range(1, 9):
                if j < 8:
                    start_sums(j, 0)
                take_start(j - 1)
                if j < 8:
                    start_sums(j, 1)
                h_low(2 * j - 2)
                h_low(2 * j - 1)
                lo_part(2 * j - 2)

            def conv(ch):
                dve.wait_ge(u_copied, ch + 1)
                o = hs[:, ch, :]
                step(dve.tensor_scalar(o, ut[:, ch, :], col(CONVW, 8 * (CW - 1) + ch), col(CONVB, ch), ALU.mult, ALU.add))
                for d in range(1, CW):
                    ins = dve.scalar_tensor_tensor(o[:, d:], ut[:, ch, 0:S - d], col(CONVW, 8 * (CW - 1 - d) + ch), o[:, d:],
                                                   ALU.mult, ALU.add)
                    if d < CW - 1:
                        step(ins)
                    else:
                        ins.then_inc(conv_done, 1)

            def one_minus_square(ch):
                dve.wait_ge(decay_ready, ch + 1)
                dve.scalar_tensor_tensor(ut[:, ch, :], a_sq[:, ch % 2, :], 1.0, ut[:, ch, :], ALU.add, ALU.mult).then_inc(m_ready, 1)

            def recurrence(ch):
                dve.wait_ge(root_ready, ch + 1)
                dve.wait_ge(ix_ready, ch + 1)
                dve.tensor_tensor(ig[:, ch, :], ut[:, ch, :], ig[:, ch, :], ALU.mult).then_inc(bx_ready, 1)
                dve.wait_ge(bx_ready, ch + 1)
                dve.tensor_tensor_scan(hs[:, ch, :], rg[:, ch, :], ig[:, ch, :], 0.0, ALU.mult, ALU.add).then_inc(scan_done, 1)

            def gate(ch):
                dve.wait_ge(gelu_done, ch + 1)
                dve.wait_ge(scan_done, ch + 1)
                dve.tensor_tensor(hs[:, ch, :], hs[:, ch, :], ut[:, ch, :], ALU.mult).then_inc(y_done, 1)

            def forget():
                dve.wait_ge(f_exp, 1)
                t = lambda i: ut[0:HEADS, i, :]
                log1p_part(t(2), t(3), t(4), t(5), t(6))
                step(dve.tensor_scalar(t(3), t(0), -1.0, 0.0, ALU.mult, ALU.max))
                step(dve.scalar_tensor_tensor(t(4), t(6), 2.0, t(3), ALU.mult, ALU.add))
                step(dve.memset(t(5), 1.0))
                dve.tensor_tensor_scan(t(7), t(5), t(4), 0.0, ALU.mult, ALU.add).then_inc(nf_ready, 1)

            for n in range(U_LAST, U_ATT + LAG):
                lo_part(n)
                for a in ada_of[n]:
                    ada_unit(a)
                e = n - U_PROJ
                if 0 <= e < CT:
                    conv(e)
                for ch in {7: [0, 1, 2, 3], 12: [4, 5, 6, 7]}.get(e, []):
                    one_minus_square(ch)
                if e == 14:
                    for ch in range(CT):
                        recurrence(ch)
                    for ch in range(4):
                        gate(ch)
                if e == 19:
                    for ch in range(4, 8):
                        gate(ch)
                if e == 31:
                    dve.wait_ge(wf_hi_ready, 1)
                    dve.tensor_tensor(wf_lo[:, :, 0:HEADS], wf_raw[:, :, :], wf_hi[:, :, 0:HEADS].bitcast(F32),
                                      ALU.subtract).then_inc(wf_lo_ready, 1)
                if e == 6 * 8 + 3:
                    forget()
                for gi in range(1, 8):
                    if e == 8 * gi + COLUMNS_AT[gi] + LAG:
                        take_columns(gi - 1, (banks[1] if gi == 6 else banks[5]) if gi >= 6 else banks[(4, 0)[gi % 2]])
                if e == 7 * 8 + 2:
                    dve.wait_ge(row_std, 1)
                    dve.reciprocal(stat[:, RL:RL + NT], stat[:, RL:RL + NT]).then_inc(row_ready, 1)
                if e == 7 * 8 + 6 + LAG:
                    take_columns(7, banks[6])

            for ch in range(CT):
                dve.wait_ge(yl_hi_ready, ch + 1)
                dve.scalar_tensor_tensor(yl_lo[:, ch, :], hs[:, ch, :], col(G_LRU, ch), yl_hi[:, ch, :].bitcast(F32),
                                         ALU.mult, ALU.subtract).then_inc(yl_lo_ready, 1)

            def softmax_rows(h):
                dve.wait_ge(nf_in[h % 2], 16 * (h // 2 + 1))
                dve.wait_ge(nfm_ready, h + 1)
                for e, i in enumerate((1, 0, 2, 3)):
                    if i != 0:
                        dve.wait_ge(score_done, 3 * h + {1: 1, 2: 2, 3: 3}[i])
                    else:
                        dve.wait_ge(score_done, 3 * h + 2)
                    b, c0 = SCORE_AT[i]
                    L = LP[:, LP_AT[i]:LP_AT[i] + (i + 1) * P]
                    if i:
                        dve.tensor_tensor(L[:, 0:i * P], b[:, c0:c0 + i * P], nF[:, h % 2, 0:i * P], ALU.add)
                    step(dve.tensor_tensor(L[:, i * P:], b[:, c0 + i * P:c0 + (i + 1) * P], nFm[:, i * P:(i + 1) * P], ALU.add))
                    dve.tensor_reduce(stat[:, NM + i:NM + i + 1], L, AX, ALU.max, negate=True).then_inc(neg_max, 1)
                dve.wait_ge(exp_done, 4 * (h + 1))
                step(dve.reciprocal(stat[:, ES:ES + NT], stat[:, ES:ES + NT]))
                for i in range(NT):
                    L = LP[:, LP_AT[i]:LP_AT[i] + (i + 1) * P]
                    dve.tensor_scalar(L, L, stat[:, ES + i:ES + i + 1], None, ALU.mult).then_inc(prob_ready, 1)

            def head_low(h):
                dve.wait_ge(ya_hi_ready, h + 1)
                dve.scalar_tensor_tensor(ya_lo[:, h, :], banks[7][:, :], col(G_ATT, h), ya_hi[:, h, :].bitcast(F32),
                                         ALU.mult, ALU.subtract).then_inc(ya_lo_ready, 1)

            for h in range(HEADS):
                softmax_rows(h)
                if h:
                    head_low(h - 1)
                lo_part(U_ATT + LAG + h)
            head_low(HEADS - 1)

            def mix_evacuation(r):
                g, _ = REST[r]
                cols = slice(g * COLS, (g + 1) * COLS)
                e = 4 * [1, 2, 3, 5].index(r)
                dve.wait_ge(unit_used, U_OUT + 4 * r + 4)
                dve.wait_ge(half_copied, {0: 4, 1: 8, 2: 12, 3: 16}[g])
                for t in range(NT):
                    dve.scalar_tensor_tensor(yg[:, t, cols], SET_Q[t][:, :] if r % 2 else SET_P[t][:, :], stat[:, RA + t:RA + t + 1],
                                             yacc[:, t, g, :] if g < 2 else yg[:, t, cols], ALU.mult, ALU.add).then_inc(y_sum, 1)
                for t in range(NT):
                    dve.wait_ge(y_sq, e + t + 1)
                    dve.tensor_tensor(yg[:, t, cols], yg[:, t, cols], G1[:, cols], ALU.mult).then_inc(y_gated, 1)

            for n in range(U_OUT + LAG, U_MLP + LAG):
                lo_part(n)
                for a in ada_of[n]:
                    ada_unit(a)
                done = n - LAG + 1 - U_OUT
                if done == 3:
                    take_gate(0, banks[5])
                    dve.wait_ge(row_std, 2)
                    step(dve.reciprocal(stat[:, RA:RA + NT], stat[:, RA:RA + NT]))
                if done in (11, 15, 19):
                    q = done // 4 - 1
                    take_gate(q, (SET_P, SET_Q)[q % 2][0])
                if done and done % 4 == 0 and REST[done // 4 - 1][1]:
                    mix_evacuation(done // 4 - 1)

            dve.wait_ge(y_gated, 16)
            dve.tensor_reduce(stat[:, YR:YR + NT], stat[:, YS:YS + 4 * NT].rearrange("p (t g) -> p t g", g=4), AX, ALU.add).then_inc(mix_sum, 1)
            dve.wait_ge(mix_std, 1)
            step(dve.reciprocal(stat[:, YR:YR + NT], stat[:, YR:YR + NT]))

            def diagonal(t):
                dve.wait_ge(x1_std, t + 1)
                step(dve.reciprocal(stat[:, X1R_ + t:X1R_ + t + 1], stat[:, X1S + t:X1S + t + 1]))
                dve.tensor_scalar(x1diag[:, t, :], ident[:, :], stat[:, X1R_ + t:X1R_ + t + 1], None, ALU.mult).then_inc(x1diag_ready, 1)

            for t in range(NT):
                dve.wait_ge(xr_in[t], 16)
                src = xr2[:, :] if t == 2 else xr[:, t % 2, :]
                dve.scalar_tensor_tensor(yg[:, t, :], yg[:, t, :], stat[:, YR + t:YR + t + 1], src, ALU.mult, ALU.add).then_inc(x1_done, 1)
                if t:
                    diagonal(t - 1)
            diagonal(NT - 1)

            def modulate(kt):
                dve.wait_ge(h2_hi_ready, kt + 1)
                if kt >= 2:
                    dve.wait_ge(h2_lo_ready, kt - 1)
                m = mtmp[:, kt % 2, :]
                step(dve.tensor_scalar(m, SET_Q[kt % 4][:, :], A2[:, kt:kt + 1], S2[:, kt:kt + 1], ALU.mult, ALU.add))
                dve.tensor_tensor(h_lo[:, kt, :], m, h_hi[:, kt, :].bitcast(F32), ALU.subtract).then_inc(h2_lo_ready, 1)

            def lo_of_chunk(ck, j):
                slot, _ = chunk_raw(ck, j)
                s = (U_MLP + j) % RING
                dve.wait_ge(hi_ready, ck * PER_CHUNK + (U_MLP + j + 1))
                dve.tensor_tensor(w_lo[:, s], raw[:, slot], w_hi[:, s].bitcast(F32), ALU.subtract).then_inc(lo_ready, 1)

            def hidden(ck, g):
                for m in range(4):
                    e = 4 * g + m
                    dve.wait_ge(relu_done, ck * 8 + (e + 1))
                    if e or not (isinstance(ck, int) and ck == 0):
                        dve.wait_ge(u_lo_ready, ck * 8 + e)
                    dve.tensor_tensor(u_full_t[:, :], rt[:, m % 2, :], rt[:, m % 2, :], ALU.mult).then_inc(u_sq, 1)
                    dve.wait_ge(u_sq, ck * 8 + (e + 1))
                    dve.wait_ge(u_hi_ready, ck * 8 + (e + 1))
                    dve.tensor_tensor(u_lo[:, e, :], u_full_t[:, :], u_hi[:, e, :].bitcast(F32), ALU.subtract).then_inc(u_lo_ready, 1)

            def add_out(ck, g, j_end, first=False):
                bank_of = (SET_P, SET_Q)[g % 2]
                cols = slice(g * COLS, (g + 1) * COLS)
                dve.wait_ge(unit_used, ck * PER_CHUNK + (U_MLP + j_end))
                if first:
                    dve.wait_ge(x1_stored, 16 * NT)
                else:
                    dve.wait_ge(y2_done, ck * 16 + 4 * g)
                for t in range(NT):
                    if first:
                        dve.tensor_copy(y2[:, t, cols], bank_of[t][:, :]).then_inc(y2_done, 1)
                    else:
                        dve.tensor_tensor(y2[:, t, cols], bank_of[t][:, :], y2[:, t, cols], ALU.add).then_inc(y2_done, 1)

            def finish_gate(g):
                for t in range(NT):
                    dve.wait_ge(f_ssq, 4 * g + t + 1)
                    cols = slice(g * COLS, (g + 1) * COLS)
                    dve.tensor_tensor(y2[:, t, cols], y2[:, t, cols], G2[:, cols], ALU.mult).then_inc(y2_gated, 1)

            def chunk(ck, j0=LAG, first=False, last=False):
                for j in range(j0, PER_CHUNK):
                    lo_of_chunk(ck, j)
                    if first:
                        for a in ada_of[U_MLP + j]:
                            ada_unit(a)
                    if j == 7 + LAG:
                        hidden(ck, 0)
                    if j == 15 + LAG:
                        hidden(ck, 1)
                    if j in (19 + LAG, 23 + LAG, 27 + LAG):
                        add_out(ck, (j - 19 - LAG) // 4, j - LAG + 1, first)
                    if first and j - LAG in GATE2_AFTER:
                        q = GATE2_AFTER.index(j - LAG)
                        take_gate(4 + q, banks[4 * (q % 2)])
                    if last and j in (20 + LAG, 24 + LAG, 28 + LAG):
                        finish_gate((j - 20 - LAG) // 4)

            def next_units(ck):
                for j in range(LAG):
                    lo_of_chunk(ck + 1, j)
                add_out(ck, 3, PER_CHUNK, isinstance(ck, int) and ck == 0)

            for kt in range(KT):
                modulate(kt)
                if kt >= 5 and kt % 2:
                    lo_of_chunk(0, LAG + (kt - 5) // 2)
                    for a in ada_of[U_MLP + LAG + (kt - 5) // 2]:
                        ada_unit(a)
            chunk(0, LAG + 6, first=True)
            next_units(0)
            with dve.Fori(1, CHUNKS - 1) as ck:
                chunk(ck)
                next_units(ck)
            chunk(CHUNKS - 1, last=True)
            add_out(CHUNKS - 1, 3, 32)
            finish_gate(3)
            dve.tensor_reduce(stat[:, FR:FR + NT], stat[:, FS:FS + 4 * NT].rearrange("p (t g) -> p t g", g=4), AX, ALU.add).then_inc(fin_sum, 1)
            dve.wait_ge(fin_std, 1)
            dve.reciprocal(stat[:, FR:FR + NT], stat[:, FR:FR + NT]).then_inc(fin_std, 1)
            dve.wait_ge(fin_std, 2)
            dve.wait_ge(y2_gated, 16)
            dve.wait_ge(x1r_in, 16 * NT)
            for t in range(NT):
                dve.scalar_tensor_tensor(x1r[:, t, :], y2[:, t, :], stat[:, FR + t:FR + t + 1], x1r[:, t, :],
                                         ALU.mult, ALU.add).then_inc(out_ready, 1)

        @block.gpsimd
        def _(pool):
            pool.memset(ident[:, :], 0.0).then_inc(pool_step, 1)
            pool.memset(causal[:, :], 0.0).then_inc(pool_step, 1)
            pool.wait_ge(pool_step, 2)
            pool.affine_select(out=ident[:, :], in_=ident[:, :], compare_op=ALU.not_equal, fill=1.0, base=0,
                               pattern=[[-1, P]], channel_multiplier=1).then_inc(const_ready, 1)
            pool.memset(ones[:, :], 1.0).then_inc(const_ready, 1)
            pool.memset(eps[:, :], EPS).then_inc(const_ready, 1)
            pool.memset(acc_init[:, :], 0.0).then_inc(const_ready, 1)
            pool.affine_select(out=causal[:, :], in_=causal[:, :], compare_op=ALU.is_ge, fill=MASKED, base=0,
                               pattern=[[-1, P]], channel_multiplier=1).then_inc(pool_step, 1)
            pool.wait_ge(x_std, 1)
            pool.memset(wrg[:, :, :], 0.0).then_inc(gw_zero, 1)
            pool.memset(wig[:, :, :], 0.0).then_inc(gw_zero, 1)
            for j in range(8):
                for kt in (2 * j, 2 * j + 1):
                    pool.wait_ge(h_hi_ready, kt + 1)
                    pool.tensor_scalar(xnT[:, kt, :], xnT[:, kt, :], A1[:, kt:kt + 1], S1[:, kt:kt + 1], ALU.mult,
                                       ALU.add).then_inc(h_sum, 1)
                slot, _, s = unit(2 * j + 1)
                pool.wait_ge(hi_ready, 2 * j + 2)
                pool.tensor_tensor(w_lo[:, s], raw[:, slot], w_hi[:, s].bitcast(F32), ALU.subtract).then_inc(lo_pool, 1)
            for ch in range(CT):
                pool.wait_ge(sig_done, 2 * ch + 2)
                pool.tensor_tensor(ig[:, ch, :], ig[:, ch, :], hs[:, ch, :], ALU.mult).then_inc(ix_ready, 1)
            for ch in range(CT):
                pool.wait_ge(y_done, ch + 1)
                if ch == 0:
                    pool.tensor_tensor(ssq[:, :], hs[:, ch, :], hs[:, ch, :], ALU.mult).then_inc(ssq_done, 1)
                else:
                    pool.wait_ge(ssq_done, ch)
                    pool.tensor_tensor(sq[:, :], hs[:, ch, :], hs[:, ch, :], ALU.mult).then_inc(pool_step, 1)
                    pool.wait_ge(pool_step, 3 + ch)
                    pool.tensor_tensor(ssq[:, :], ssq[:, :], sq[:, :], ALU.add).then_inc(ssq_done, 1)
            pool.wait_ge(ssq_done, CT)
            pool.memset(wf_hi[:, :, :].bitcast(F32), 0.0).then_inc(wf_zero, 1)
            pool.memset(wf_lo[:, :, :].bitcast(F32), 0.0).then_inc(wf_zero, 1)

            def load_nf(h):
                if h >= 2:
                    pool.wait_ge(neg_max, 4 * (h - 1))
                    pool.wait_ge(nfm_ready, h - 1)
                pool.dma_start(nF[:, h % 2, :], f_scr[h:h + 1, :].to_broadcast([P, S])).then_inc(nf_in[h % 2], 16)

            def mask_nf(h):
                pool.wait_ge(nf_in[h % 2], 16 * (h // 2 + 1))
                if h:
                    pool.wait_ge(neg_max, 4 * h)
                pool.tensor_tensor(nFm[:, :].rearrange("p (i k) -> p i k", k=P), nF[:, h % 2, :].rearrange("p (i k) -> p i k", k=P),
                                   causal[:, :].unsqueeze(1).to_broadcast([P, NT, P]), ALU.add).then_inc(nfm_ready, 1)

            pool.wait_ge(nf_ready, 1)
            pool.dma_start(f_scr[:, :], ut[0:HEADS, 7, :]).then_inc(nf_stored, 16)
            pool.wait_ge(nf_stored, 16)
            load_nf(0)
            load_nf(1)
            pool.wait_ge(pool_step, 2 + CT)
            mask_nf(0)
            for h in range(HEADS):
                if h + 1 < HEADS:
                    mask_nf(h + 1)
                if h + 2 < HEADS:
                    load_nf(h + 2)
                pool.wait_ge(ya_sq, h + 1)
                if h == 0:
                    pool.wait_ge(row_done, 1)
                    pool.tensor_copy(ssq[:, :], g_row[:, :]).then_inc(att_ssq, 1)
                else:
                    pool.wait_ge(att_ssq, h)
                    pool.tensor_tensor(ssq[:, :], ssq[:, :], g_row[:, :], ALU.add).then_inc(att_ssq, 1)

            def load_gain(q):
                pool.wait_ge(gate_ready, q) if q else pool.wait_ge(att_ssq, HEADS)
                g = (g_post_mix, g_post_mlp)[q // 4]
                pool.dma_start(g_row[:, :], g[0:1, q % 4 * COLS:(q % 4 + 1) * COLS].to_broadcast([P, COLS])).then_inc(gain_in, 16)

            def load_x(t):
                dst = xr2[:, :] if t == 2 else xr[:, t % 2, :]
                pool.dma_start(dst, x2[t * P:(t + 1) * P, :]).then_inc(xr_in[t], 16)

            load_gain(0)
            pool.wait_ge(pv_done, HEADS)
            load_x(2)
            load_gain(1)
            pool.wait_ge(y_sum, 8)
            load_x(0)
            load_x(1)
            for q in (2, 3, 4):
                load_gain(q)
            for t in range(NT):
                pool.wait_ge(x1_done, t + 1)
                pool.dma_start(x1_scr[t * P:(t + 1) * P, :], yg[:, t, :]).then_inc(x1_stored, 16)
                if t == 1:
                    load_x(3)
            for q in (5, 6, 7):
                load_gain(q)
            pool.wait_ge(x1_stored, 16 * NT)
            pool.wait_ge(unit_used, U_MLP + (CHUNKS - 1) * PER_CHUNK + 16)
            for t in range(NT):
                pool.dma_start(x1r[:, t, :], x1_scr[t * P:(t + 1) * P, :]).then_inc(x1r_in, 16)

    return nc


_INS = ['x', 'c', 'w_ada', 'b_ada', 'g_pre_mix', 'g_post_mix', 'g_pre_mlp', 'g_post_mlp', 'w_in', 'conv_w', 'conv_b',
        'w_rg', 'b_rg', 'w_ig', 'b_ig', 'lru_lambda', 'b_forget', 'g_lru_out', 'g_att_out', 'w_out', 'w_ff1', 'w_ff2']


def kernel(**inputs):
    import numpy as _np
    import concourse.bacc as _bacc
    from concourse import mybir as _mybir
    from concourse.bass_utils import run_bass_kernel_spmd as _run

    nc = _bacc.Bacc("TRN2", target_bir_lowering=False, num_devices=1)
    arrays, args = {}, []
    for name in _INS:
        a = _np.ascontiguousarray(inputs[name])
        arrays[f"in_{name}_dram"] = a
        args.append(nc.dram_tensor(f"in_{name}_dram", a.shape, _mybir.dt.from_np(a.dtype), kind="ExternalInput").ap())
    shape = tuple(inputs["x"].shape)
    args.append(nc.dram_tensor("out_0_dram", shape, _mybir.dt.float32, kind="ExternalOutput").ap())
    hybrid_layer(nc, *args)
    r = _run(nc, [arrays], core_ids=[0])
    return r.results[0]["out_0_dram"]
```

```python
from contextlib import ExitStack

import concourse.bass as bass
from concourse import mybir

F32 = mybir.dt.float32
F32R = mybir.dt.float32r
ALU = mybir.AluOpType
ACT = mybir.ActivationFunctionType
AX = mybir.AxisListType.X

P = 128
EPS = 1e-6
LRU_C = 8.0
MASKED = -1e30
RING = 4
COLS = 512
LAG = 3


def hybrid_layer(nc, x, c, w_ada, b_ada, g_pre_mix, g_post_mix, g_pre_mlp, g_post_mlp, w_in, conv_w, conv_b,
                 w_rg, b_rg, w_ig, b_ig, lru_lambda, b_forget, g_lru_out, g_att_out, w_out, w_ff1, w_ff2, out):
    S, D = x.shape[1], x.shape[2]
    D_LRU, D_ATT, D_FF = conv_b.shape[1], g_att_out.shape[1], w_ff1.shape[2]
    HEADS = b_forget.shape[1]
    DH = D_ATT // HEADS
    CW = conv_w.shape[1]
    LB = w_rg.shape[2]
    KT = D // P
    NT = S // P
    CT = D_LRU // P
    CHUNKS = 8
    FT = D_FF // CHUNKS // P
    assert (S, D, DH, KT, NT, CT, FT, CW, HEADS, LB) == (512, 2048, 128, 16, 4, 8, 8, 4, 8, 64)

    x2 = x.rearrange("b s d -> (b s) d")
    out2 = out.rearrange("b s d -> (b s) d")
    w_ada2, w_in2, w_out2, w_ff12, w_ff22 = (w.rearrange("l k n -> (l k) n") for w in (w_ada, w_in, w_out, w_ff1, w_ff2))

    U_LAST = 2 * KT // 2
    U_PROJ = U_LAST + 2
    U_ATT = U_PROJ + 8 * 8
    U_OUT = U_ATT + HEADS
    U_MLP = U_OUT + 24
    PER_CHUNK = 32
    U_LOOP = U_MLP + PER_CHUNK
    REST = [(2, 0), (0, 1), (1, 1), (2, 1), (3, 0), (3, 1)]

    def ada_after(n):
        if U_PROJ <= n < U_ATT:
            return 1 + (n >= U_ATT - 8)
        return (U_ATT + 2 <= n < U_OUT + 2) + (U_OUT + 3 <= n < U_OUT + 19) + 2 * (U_MLP + 8 <= n < U_MLP + 24)

    stream, main_pos, ada_pos, ada_of = [], {}, {}, {}
    for n in range(U_LOOP):
        main_pos[n] = len(stream)
        stream.append(("w", n))
        ada_of[n] = []
        for _ in range(ada_after(n)):
            a = len(ada_pos)
            ada_of[n].append(a)
            ada_pos[a] = len(stream)
            stream.append(("ada", a))
    POS_LOOP = len(stream)
    assert len(ada_pos) == 16 * 8 and PER_CHUNK % RING == 0
    COLUMNS_AT = {1: 6, 2: 4, 3: 4, 4: 4, 5: 4, 6: 4, 7: 2}
    ADA_COL = [base * D + g * COLS for base in (4, 3, 2, 5) for g in range(4)]

    def place(pos):
        return pos % RING, 16 * (pos // RING + 1)

    def chunk_raw(ck, j):
        if isinstance(ck, int) and ck == 0:
            return place(main_pos[U_MLP + j])
        slot, count = place(POS_LOOP + j)
        return slot, count + (ck - 1) * (16 * PER_CHUNK // RING)

    def unit(n):
        return (*place(main_pos[n]), n % RING)

    def lo_count(n):
        return n // 2 + 1 if n < U_LAST else n - 7

    with ExitStack() as ctx:
        def sb(name, shape, dt=F32):
            return ctx.enter_context(nc.sbuf_tensor(name, shape, dt))

        def sem(name):
            return ctx.enter_context(nc.semaphore(name))

        def overlay(*specs):
            with ExitStack() as phase:
                return [phase.enter_context(nc.sbuf_tensor(n, s, d)) for n, s, d in specs]

        raw = sb("raw", [P, RING, 2 * COLS])
        w_hi = sb("w_hi", [P, RING, 2 * COLS], F32R)
        w_lo = sb("w_lo", [P, RING, 2 * COLS], F32R)
        ident = sb("ident", [P, P])
        ones = sb("ones", [P, P])
        causal = sb("causal", [P, P])
        vrow = sb("vrow", [P, P])
        vcol = sb("vcol", [P, 112])
        acc = sb("acc", [P, 2, COLS])
        acc_init = sb("acc_init", [P, COLS])
        g_row = sb("g_row", [P, COLS])
        ssq = sb("ssq", [P, COLS])
        cc = sb("cc", [P, 4, KT])
        A1, S1, A2, S2 = (sb(n, [P, KT]) for n in ("A1", "S1", "A2", "S2"))
        stat = sb("stat", [P, 96])
        lam = sb("lam", [P, 8, CT])
        wf_raw = sb("wf_raw", [P, KT, HEADS])
        bf = sb("bf", [HEADS, 1])
        eps = sb("eps", [P, 1])
        mod = sb("mod", [P, 4])

        G_PRE_MIX, G_PRE_MLP, CONVW, CONVB, B_RG, B_IG, LAMBDA, G_LRU, G_ATT = 0, 16, 32, 64, 72, 80, 88, 96, 104

        h_hi, x_tok, gst0, xnT, gst1, junk = overlay(
            ("h_hi", [P, KT, COLS], F32R), ("x_tok", [P, NT, D], F32), ("gst0", [P, 8, 2, 256], F32),
            ("xnT", [P, KT, COLS], F32), ("gst1", [P, 8, 2, 256], F32), ("junk", [P, D], F32))
        _, h_lo, hs, rg, ig, ut, wrg, wig, a_sq, sq = overlay(
            ("pad2", [P, KT, COLS], F32), ("h_lo", [P, KT, COLS], F32R), ("hs", [P, CT, COLS], F32),
            ("rg", [P, CT, COLS], F32), ("ig", [P, CT, COLS], F32), ("ut", [P, CT, COLS], F32),
            ("wrg", [P, CT, P], F32), ("wig", [P, CT, P], F32), ("a_sq", [P, 2, COLS], F32), ("sq", [P, COLS], F32))
        yl_hi, yl_lo, ya_hi, ya_lo, yacc, qT, kT, vv, LP, PT, nF, nFm = overlay(
            ("yl_hi", [P, CT, COLS], F32R), ("yl_lo", [P, CT, COLS], F32R), ("ya_hi", [P, HEADS, COLS], F32R),
            ("ya_lo", [P, HEADS, COLS], F32R), ("yacc", [P, NT, 2, COLS], F32), ("qT", [P, HEADS, S], F32),
            ("kT", [P, HEADS, S], F32), ("vv", [P, NT, D_ATT], F32), ("LP", [P, 1280], F32), ("PT", [P, 1280], F32),
            ("nF", [P, 2, S], F32), ("nFm", [P, S], F32))
        _, x1T = overlay(("pad7", [P, KT, COLS], F32), ("x1T", [P, KT, COLS], F32))
        *_, wf_hi, wf_lo = overlay(("pad3", [P, 128 * 256], F32), ("wf_hi", [P, KT, P], F32R), ("wf_lo", [P, KT, P], F32R))
        _, xr, yg, G1, xr2, x1diag, junk2 = overlay(
            ("pad4", [P, 64 * 256], F32), ("xr", [P, 2, D], F32), ("yg", [P, NT, D], F32), ("G1", [P, D], F32),
            ("xr2", [P, D], F32), ("x1diag", [P, NT, P], F32), ("junk2", [P, D], F32))
        x1r, _, u_hi, _, u_lo, G2, rt, u_full_t, junk3 = overlay(
            ("x1r", [P, NT, D], F32), ("pad5", [P, 32 * 256], F32), ("u_hi", [P, FT, COLS], F32R),
            ("pad6", [P, 32 * 256], F32), ("u_lo", [P, FT, COLS], F32R), ("G2", [P, D], F32),
            ("rt", [P, 2, COLS], F32), ("u_full_t", [P, COLS], F32), ("junk3", [P, COLS], F32))
        gst = [(gst0, gst1)[q // 2][:, q % 2 * 4:q % 2 * 4 + 4] for q in range(4)]
        y2 = yg

        banks = [ctx.enter_context(nc.psum_tensor(f"bank{b}", [P, COLS], F32)) for b in range(8)]
        SET_P, SET_Q = banks[:4], banks[4:]

        f_scr = nc.dram_tensor("f_scratch", [HEADS, S], F32, kind="Internal").ap()
        x1_scr = nc.dram_tensor("x1_scratch", [S, D], F32, kind="Internal").ap()

        raw_in = [sem(f"raw_in{i}") for i in range(RING)]
        hi_ready = sem("hi_ready")
        lo_ready = sem("lo_ready")
        lo_pool = sem("lo_pool")
        unit_used = sem("unit_used")
        ada_used = sem("ada_used")
        vec_in, c_in, bf_in, wf_in, gw_in = (sem(n) for n in ("vec_in", "c_in", "bf_in", "wf_in", "gw_in"))
        x_in = [sem(f"x_in{t}") for t in range(NT)]
        gst_in = [sem(f"gst_in{i}") for i in range(4)]
        gst_used = sem("gst_used")
        init_in = sem("init_in")
        acc_first = sem("acc_first")
        acc_read = sem("acc_read")
        mod_read = sem("mod_read")
        gain_in = sem("gain_in")
        gate_ready = sem("gate_ready")
        const_ready = sem("const_ready")
        vec_turned, vcol_ready = sem("vec_turned"), sem("vcol_ready")
        c_exp, dve_step, act_step, pool_step = (sem(n) for n in ("c_exp", "dve_step", "act_step", "pool_step"))
        lam_exp, kp_ready = sem("lam_exp"), sem("kp_ready")
        x_ssq, x_std, x_scaled, xt_done, xt_copied = (sem(n) for n in ("x_ssq", "x_std", "x_scaled", "xt_done", "xt_copied"))
        h_hi_ready, h_sum, h_lo_ready = (sem(n) for n in ("h_hi_ready", "h_sum", "h_lo_ready"))
        u_copied, conv_done, z_done, sig_done = (sem(n) for n in ("u_copied", "conv_done", "z_done", "sig_done"))
        decay_ready, m_ready, root_ready, ix_ready, bx_ready, scan_done, gelu_done, y_done, ssq_done = (
            sem(n) for n in ("decay_ready", "m_ready", "root_ready", "ix_ready", "bx_ready", "scan_done", "gelu_done",
                             "y_done", "ssq_done"))
        q_copied, k_copied, v_copied = sem("q_copied"), sem("k_copied"), sem("v_copied")
        wf_zero, wf_hi_ready, wf_lo_ready, f_done, f_read, f_exp = (
            sem(n) for n in ("wf_zero", "wf_hi_ready", "wf_lo_ready", "f_done", "f_read", "f_exp"))
        nf_ready, nf_stored, nfm_ready = sem("nf_ready"), sem("nf_stored"), sem("nfm_ready")
        nf_in = [sem(f"nf_in{i}") for i in range(2)]
        row_done, row_std, row_ready = sem("row_done"), sem("row_std"), sem("row_ready")
        yl_hi_ready, yl_lo_ready = sem("yl_hi_ready"), sem("yl_lo_ready")
        score_done, score_read, neg_max, exp_done, prob_ready, pt_done, pt_copied, pv_done = (
            sem(n) for n in ("score_done", "score_read", "neg_max", "exp_done", "prob_ready", "pt_done", "pt_copied", "pv_done"))
        ya_sq, ya_hi_ready, ya_lo_ready, att_ssq = (sem(n) for n in ("ya_sq", "ya_hi_ready", "ya_lo_ready", "att_ssq"))
        half_copied, y_sum, y_sq, y_gated = (sem(n) for n in ("half_copied", "y_sum", "y_sq", "y_gated"))
        mix_std, mix_sum, fin_sum = sem("mix_std"), sem("mix_sum"), sem("fin_sum")
        gw_zero = sem("gw_zero")
        xr_in = [sem(f"xr_in{t}") for t in range(NT)]
        x1_done, x1_ssq, x1_std, x1diag_ready, x1_stored = (sem(n) for n in ("x1_done", "x1_ssq", "x1_std", "x1diag_ready", "x1_stored"))
        x1t_done, x1t_copied, h2_hi_ready, h2_sum, h2_lo_ready = (
            sem(n) for n in ("x1t_done", "x1t_copied", "h2_hi_ready", "h2_sum", "h2_lo_ready"))
        mix_tile, out_tile = sem("mix_tile"), sem("out_tile")
        relu_done, u_sq, u_hi_ready, u_lo_ready, y2_done = (sem(n) for n in ("relu_done", "u_sq", "u_hi_ready", "u_lo_ready", "y2_done"))
        x1r_in = sem("x1r_in")
        f_ssq, y2_gated, fin_std, out_ready, stored = (sem(n) for n in ("f_ssq", "y2_gated", "fin_std", "out_ready", "stored"))

        XS, XR, RL, RA, YS, YR, X1S, X1R_, FS, FR, NM, ES = 0, 4, 8, 12, 16, 32, 40, 44, 48, 64, 72, 80

        def col(base, i=0, n=1):
            return vcol[:, base + i:base + i + n]

        block = ctx.enter_context(nc.Block())

        SCORE_AT = {3: (banks[4], 0), 2: (banks[5], 0), 0: (banks[5], 3 * P), 1: (banks[6], 0)}
        LP_AT = [0, P, 3 * P, 6 * P]
        PT_PSUM = {0: (banks[4], 0), 1: (banks[5], 0), 3: (banks[5], 3 * P), 2: (banks[6], 0)}
        PT_AT = {0: 0, 1: 4 * P, 3: 7 * P, 2: 8 * P}
        GATE2_AFTER = (12, 17, 21, 26)

        @block.sync
        def _(sp):
            def slot_free(pos):
                if pos < RING:
                    return
                kind, n = stream[pos - RING]
                if kind == "ada":
                    sp.wait_ge(ada_used, n + 1)
                elif n < U_LAST and n % 2:
                    sp.wait_ge(lo_pool, n // 2 + 1)
                else:
                    sp.wait_ge(lo_ready, lo_count(n))

            def rows(w, r0, c0, tall=2, cols=COLS):
                return w[r0:r0 + tall * P, c0:c0 + cols].rearrange("(k p) n -> p k n", p=P)

            def source(n):
                if n < U_LAST:
                    return rows(w_in2, n // 2 * 2 * P, n % 2 * COLS)
                if n < U_PROJ:
                    return rows(w_in2, (n - U_LAST) * 8 * P, (CT - 1) * P, 8, P)
                if n < U_ATT:
                    g, v = divmod(n - U_PROJ, 8)
                    return rows(w_in2, v * 2 * P, D_LRU + g * COLS)
                if n < U_OUT:
                    g, v = divmod(n - U_ATT, 4)
                    return rows(w_out2, v * 2 * P, g * COLS)
                if n < U_MLP:
                    r, v = divmod(n - U_OUT, 4)
                    g, half = REST[r]
                    return rows(w_out2, half * D_LRU + v * 2 * P, g * COLS)
                return mlp_source(0, n - U_MLP)

            def mlp_source(ck, j):
                if j < 16:
                    g, v = divmod(j, 8)
                    return w_ff12[v * 2 * P:(v + 1) * 2 * P, bass.ds(ck * (FT * P) + g * COLS, COLS)].rearrange("(k p) n -> p k n", p=P)
                g, v = divmod(j - 16, 4)
                return w_ff22[bass.ds(ck * (FT * P) + v * 2 * P, 2 * P), g * COLS:(g + 1) * COLS].rearrange("(k p) n -> p k n", p=P)

            def load_init(m):
                if m:
                    sp.wait_ge(acc_first, m)
                parts = ((D + m * 256, 0, 256), (m * 256, 256, 256)) if m < 8 else ((ADA_COL[m - 8], 0, COLS),)
                for c0, at, width in parts:
                    sp.dma_start(acc_init[0:1, at:at + width], b_ada[0:1, c0:c0 + width]).then_inc(init_in, 16)

            def load(pos):
                slot, _ = place(pos)
                kind, n = stream[pos]
                if kind == "ada" and n % 8 == 0:
                    load_init(8 + n // 8)
                slot_free(pos)
                if kind == "ada":
                    cg, r = divmod(n, 8)
                    src = w_ada2[:, ADA_COL[cg]:ADA_COL[cg] + COLS].rearrange("(p k) n -> p k n", p=P)[:, 2 * r:2 * r + 2]
                else:
                    src = source(n)
                dst = raw[:, slot].rearrange("p (k n) -> p k n", k=src.shape[1])
                sp.dma_start(dst, src).then_inc(raw_in[slot], 16)

            def start_quarter(j, q):
                i = 4 * j + q
                if q == 0:
                    load_init(j)
                if i >= 4:
                    sp.wait_ge(gst_used, i - 3)
                for part, base in enumerate((D, 0)):
                    src = w_ada2[:, base + j * 256:base + (j + 1) * 256].rearrange("(p k) n -> p k n", p=P)
                    sp.dma_start(gst[q][:, :, part, :], src[:, 4 * q:4 * q + 4]).then_inc(gst_in[q], 16)

            for t in range(NT):
                sp.dma_start(x_tok[:, t], x2[t * P:(t + 1) * P, :]).then_inc(x_in[t], 16)
            sp.wait_ge(const_ready, 4)
            for j in range(8):
                for q in range(4):
                    start_quarter(j, q)
                for n in (2 * j, 2 * j + 1):
                    load(main_pos[n])
            for pos in range(main_pos[U_LAST], POS_LOOP):
                load(pos)

            def chunk(ck):
                for j in range(PER_CHUNK):
                    slot, _ = chunk_raw(1, j)
                    sp.wait_ge(lo_ready, ck * PER_CHUNK + (U_MLP + j - RING - 7))
                    sp.dma_start(raw[:, slot].rearrange("p (k n) -> p k n", k=2), mlp_source(ck, j)).then_inc(raw_in[slot], 16)

            with sp.Fori(1, CHUNKS - 1) as ck:
                chunk(ck)
            chunk(CHUNKS - 1)
            for t in range(NT):
                for half in range(2):
                    sp.wait_ge(out_ready, 2 * t + half + 1)
                    cols = slice(half * (D // 2), (half + 1) * (D // 2))
                    sp.dma_start(out2[t * P:(t + 1) * P, cols], x1r[:, t, cols]).then_inc(stored, 16)
            sp.wait_ge(stored, 16 * 2 * NT)

        @block.tensor
        def _(pe):
            def unit_ready(n):
                if n < U_LAST and n % 2:
                    pe.wait_ge(lo_pool, n // 2 + 1)
                else:
                    pe.wait_ge(lo_ready, lo_count(n))

            def w_tile(slot, k, width=COLS):
                return (w_hi[:, slot, k * width:(k + 1) * width], w_lo[:, slot, k * width:(k + 1) * width])

            def feature_major(bank_of, w, act_hi, act_lo, kt, n_kt, blocks=range(4)):
                hi, lo = w
                for m in blocks:
                    b, cols = bank_of[m], slice(m * P, (m + 1) * P)
                    pe.matmul(b[:, :], lo[:, cols], act_hi[:, kt, :], start=(kt == 0), stop=False)
                    pe.matmul(b[:, :], hi[:, cols], act_lo[:, kt, :], start=False, stop=False)
                    last = pe.matmul(b[:, :], hi[:, cols], act_hi[:, kt, :], start=False, stop=(kt == n_kt - 1))
                return last

            def token_major(bank_of, w, act_hi, act_lo, kt, n_kt, tiles=range(NT)):
                hi, lo = w
                for t in tiles:
                    b, tok = bank_of[t], slice(t * P, (t + 1) * P)
                    pe.matmul(b[:, :], act_lo[:, kt, tok], hi, start=(kt == 0), stop=False)
                    pe.matmul(b[:, :], act_hi[:, kt, tok], lo, start=False, stop=False)
                    last = pe.matmul(b[:, :], act_hi[:, kt, tok], hi, start=False, stop=(kt == n_kt - 1))
                return last

            def sums_ready(m):
                if m < 8:
                    pe.wait_ge(gst_used, 4 * (m + 1))
                else:
                    pe.wait_ge(ada_used, 8 * (m - 7))

            def column_job(m, bank):
                sums_ready(m)
                for b in range(4):
                    block_ = acc[:, m % 2, b * P:(b + 1) * P]
                    if m < 8:
                        last = pe.matmul(bank[:, b:b + 1], block_, ones[:, 0:1], start=True, stop=True)
                    else:
                        last = pe.transpose(bank[:, b * P:(b + 1) * P], block_, ident[:, :])
                last.then_inc(acc_read, 1)

            def row_job(m, bank):
                sums_ready(m)
                pe.matmul(bank[:, :], ones[:, :], acc[:, m % 2, :], start=True, stop=True).then_inc(acc_read, 1)

            def stats_job(bank):
                for t in range(NT):
                    last = pe.matmul(bank[:, t:t + 1], ssq[:, t * P:(t + 1) * P], ones[:, 0:1], start=True, stop=True)
                last.then_inc(row_done, 1)

            pe.wait_ge(const_ready, 1)
            for t in range(NT):
                pe.wait_ge(x_scaled, t + 1)
                if t >= 2:
                    pe.wait_ge(xt_copied, 4 * (t - 1))
                for kt in range(KT):
                    last = pe.transpose(banks[4 * (t % 2) + kt // 4][:, kt % 4 * P:(kt % 4 + 1) * P],
                                        x_tok[:, t, kt * P:(kt + 1) * P], ident[:, :])
                    if kt % 4 == 3:
                        last.then_inc(xt_done, 1)
            pe.wait_ge(const_ready, 2)
            pe.wait_ge(vec_in, 16 * 9)
            pe.wait_ge(xt_copied, KT)
            pe.transpose(banks[7][:, 0:112], vrow[0:112, :], ident[0:112, 0:112]).then_inc(vec_turned, 1)

            pe.wait_ge(vcol_ready, 1)
            column_job(0, banks[7])
            for j in range(8):
                for n, group, blocks in ((2 * j, SET_P, range(4)), (2 * j + 1, SET_Q, range(3))):
                    unit_ready(n)
                    for k in range(2):
                        pe.wait_ge(h_lo_ready, 2 * j + k + 1)
                        last = feature_major(group, w_tile(n % RING, k), h_hi, h_lo, 2 * j + k, KT, blocks)
                    last.then_inc(unit_used, 1)
                    if n == 2 * j and j + 1 < 8:
                        pe.wait_ge(mod_read, j + 1)
                        column_job(j + 1, banks[7])
            pe.wait_ge(mod_read, 8)
            for n in (U_LAST, U_LAST + 1):
                unit_ready(n)
                for k in range(8):
                    last = feature_major([banks[7]], w_tile(n % RING, k, P), h_hi, h_lo, 8 * (n - U_LAST) + k, KT, range(1))
                last.then_inc(unit_used, 1)

            def gates(ch):
                pe.wait_ge(conv_done, ch + 1)
                if ch < 2:
                    pe.wait_ge(u_copied, 6 + 2 * ch)
                else:
                    pe.wait_ge(sig_done, 2 * (ch - 1))
                b = 4 + 2 * (ch % 2)
                pe.matmul(banks[b][:, :], wrg[:, ch, :], hs[:, ch, :], start=True, stop=True)
                pe.matmul(banks[b + 1][:, :], wig[:, ch, :], hs[:, ch, :], start=True, stop=True).then_inc(z_done, 1)

            def scores(h):
                if h == 0:
                    pe.wait_ge(q_copied, HEADS)
                    pe.wait_ge(k_copied, HEADS)
                    pe.wait_ge(v_copied, 4)
                    pe.wait_ge(mod_read, 8 + 7)
                else:
                    pe.wait_ge(pt_copied, 3 * h)
                for i in (1, 0, 2, 3):
                    n_keys = (i + 1) * P
                    b, c0 = SCORE_AT[i]
                    last = pe.matmul(b[:, c0:c0 + n_keys], qT[:, h, i * P:(i + 1) * P], kT[:, h, 0:n_keys], start=True, stop=True)
                    if i != 0:
                        last.then_inc(score_done, 1)

            GATES_AFTER = {U_PROJ: [0], U_PROJ + 1: [1], U_PROJ + 2: [2], U_PROJ + 3: [3], U_PROJ + 5: [4, 5], U_PROJ + 7: [6, 7]}
            pe.wait_ge(gw_in, 64)
            for gi in range(8):
                bank_of = (SET_P, SET_Q)[gi % 2]
                other = (SET_Q, SET_P)[gi % 2][0]
                if gi >= 2:
                    pe.wait_ge(mod_read, 8 + gi - 1)
                if gi == 0:
                    pe.wait_ge(u_copied, 4)
                elif gi == 1:
                    pe.wait_ge(sig_done, 16)
                elif gi in (2, 3):
                    pe.wait_ge(gelu_done, 4 * (gi - 1))
                elif gi in (4, 5):
                    pe.wait_ge(q_copied, 4 * (gi - 3))
                else:
                    bank_of = (SET_Q, SET_P)[gi % 2]
                    other = (SET_P, SET_Q)[gi % 2][1]
                    if gi == 6:
                        pe.wait_ge(k_copied, 4)
                        pe.wait_ge(wf_lo_ready, 1)
                        for kt in range(KT):
                            last = feature_major([banks[0]], (wf_hi[:, kt, :], wf_lo[:, kt, :]), h_hi, h_lo, kt, KT, range(1))
                        last.then_inc(f_done, 1)
                        pe.wait_ge(k_copied, 8)
                    else:
                        pe.wait_ge(f_read, 1)
                        pe.wait_ge(row_std, 1)
                for v in range(8):
                    n = U_PROJ + 8 * gi + v
                    unit_ready(n)
                    for k in range(2):
                        w = w_tile(n % RING, k)
                        if gi < 6:
                            last = feature_major(bank_of, w, h_hi, h_lo, 2 * v + k, KT)
                        else:
                            last = token_major(bank_of, w, h_hi, h_lo, 2 * v + k, KT)
                    last.then_inc(unit_used, 1)
                    for ch in GATES_AFTER.get(n, []):
                        gates(ch)
                    if gi and v == COLUMNS_AT[gi]:
                        for s, count in {1: [(gelu_done, 4)], 2: [(gelu_done, 8)], 3: [(q_copied, 4)], 4: [(q_copied, 8)],
                                         5: [(k_copied, 4)], 6: [(k_copied, 4)], 7: [(v_copied, 4)]}[gi]:
                            pe.wait_ge(s, count)
                        column_job(8 + gi - 1, other)
                    if gi == 6 and v == 6:
                        pe.wait_ge(ssq_done, CT)
                        stats_job(banks[2])
                    if gi == 7 and v == 5:
                        scores(0)
                    if gi == 7 and v == 6:
                        column_job(8 + 7, banks[7])

            def turn_probs(h):
                pe.wait_ge(prob_ready, 4 * (h + 1))
                for j in (2, 1, 3, 0):
                    b, c0 = PT_PSUM[j]
                    for i in range(j, NT):
                        last = pe.transpose(b[:, c0 + (i - j) * P:c0 + (i - j + 1) * P],
                                            LP[:, LP_AT[i] + j * P:LP_AT[i] + (j + 1) * P], ident[:, :])
                    if j != 1:
                        last.then_inc(pt_done, 1)

            def weigh_values(h):
                pe.wait_ge(pt_copied, 3 * (h + 1))
                if h == 0:
                    pe.wait_ge(v_copied, 8)
                    pe.wait_ge(mod_read, 8 + 8)
                else:
                    pe.wait_ge(ya_lo_ready, h)
                for j in range(NT):
                    last = pe.matmul(banks[7][:, j * P:S], vv[:, j, h * P:(h + 1) * P], PT[:, PT_AT[j]:PT_AT[j] + S - j * P],
                                     start=(j == 0), stop=(j == NT - 1))
                last.then_inc(pv_done, 1)

            def beside_attention(h, k):
                g, v = divmod(h, 4)
                n = U_ATT + h
                if k == 0:
                    unit_ready(n)
                    if v == 0:
                        pe.wait_ge(v_copied, 8) if g == 0 else pe.wait_ge(half_copied, 4)
                pe.wait_ge(yl_lo_ready, 2 * v + k + 1)
                last = token_major(SET_P, w_tile(n % RING, k), yl_hi, yl_lo, 2 * v + k, CT)
                if k:
                    last.then_inc(unit_used, 1)

            for h in range(HEADS):
                beside_attention(h, 0)
                turn_probs(h)
                beside_attention(h, 1)
                if h < HEADS - 1:
                    scores(h + 1)
                weigh_values(h)

            for r, (g, half) in enumerate(REST):
                bank_of = (SET_P, SET_Q)[r % 2]
                if r == 0:
                    pe.wait_ge(half_copied, 8)
                elif r == 1:
                    pe.wait_ge(ya_lo_ready, HEADS)
                    pe.wait_ge(row_std, 2)
                    pe.wait_ge(gate_ready, 1)
                elif r == 2:
                    pe.wait_ge(half_copied, 12)
                    pe.wait_ge(gate_ready, 2)
                else:
                    pe.wait_ge(y_sum, 4 * (r - 2))
                    pe.wait_ge(gate_ready, r - 1)
                act_hi, act_lo = ((yl_hi, yl_lo), (ya_hi, ya_lo))[half]
                if r < len(REST) - 1:
                    for v in range(4):
                        n = U_OUT + 4 * r + v
                        unit_ready(n)
                        for k in range(2):
                            last = token_major(bank_of, w_tile(n % RING, k), act_hi, act_lo, 2 * v + k, CT)
                        last.then_inc(unit_used, 1)
                        if r == 0 and v == 1:
                            pe.wait_ge(att_ssq, HEADS)
                            stats_job(banks[4])
                        if v == (0, 2, None, 2, 2)[r]:
                            if r == 0:
                                pe.wait_ge(pt_copied, 3 * HEADS)
                            elif r == 1:
                                pe.wait_ge(half_copied, 12)
                            else:
                                pe.wait_ge(y_sum, 4 * (r - 1))
                            row_job(16 + (0, 1, None, 2, 3)[r], banks[5] if r == 0 else (SET_Q, SET_P)[r % 2][0])
                    continue
                for t in range(NT):
                    for v in range(4):
                        n = U_OUT + 4 * r + v
                        unit_ready(n)
                        for k in range(2):
                            last = token_major(bank_of, w_tile(n % RING, k), act_hi, act_lo, 2 * v + k, CT, [t])
                        if t == NT - 1:
                            last.then_inc(unit_used, 1)
                        elif v == 3:
                            last.then_inc(mix_tile, 1)

            for t in range(NT):
                pe.wait_ge(x1diag_ready, t + 1)
                if t == 0:
                    pe.wait_ge(half_copied, 16)
                elif t == 1:
                    pe.wait_ge(y_sum, 16)
                else:
                    pe.wait_ge(x1t_copied, 4 * (t - 1))
                for kt in range(KT):
                    last = pe.matmul((SET_P, SET_Q)[t % 2][kt // 4][:, kt % 4 * P:(kt % 4 + 1) * P], yg[:, t, kt * P:(kt + 1) * P],
                                     x1diag[:, t, :], start=(kt % 4 == 0), stop=(kt % 4 == 3))
                    if kt % 4 == 3:
                        last.then_inc(x1t_done, 1)

            def chunk(ck, first=False, last_chunk=False):
                n_of = lambda j: U_MLP + j
                slot_of = lambda j: (U_MLP + j) % RING
                if first:
                    pe.wait_ge(x1t_copied, 4 * (NT - 1))
                else:
                    pe.wait_ge(y2_done, ck * 16 - 4)
                for j in range(PER_CHUNK - 4 * last_chunk):
                    if j == 8:
                        pe.wait_ge(x1t_copied, 4 * NT) if first else pe.wait_ge(y2_done, ck * 16)
                    elif j == 16:
                        pe.wait_ge(relu_done, ck * 8 + 4)
                        if first:
                            pe.wait_ge(gate_ready, 5)
                    elif j == 20:
                        pe.wait_ge(relu_done, ck * 8 + 8)
                        if first:
                            pe.wait_ge(gate_ready, 6)
                    elif j == 24:
                        pe.wait_ge(y2_done, ck * 16 + 4)
                        if first:
                            pe.wait_ge(gate_ready, 7)
                    elif j == 28:
                        pe.wait_ge(y2_done, ck * 16 + 8)
                        if first:
                            pe.wait_ge(gate_ready, 8)
                    pe.wait_ge(lo_ready, ck * PER_CHUNK + (n_of(j) - 7))
                    for k in range(2):
                        w = w_tile(slot_of(j), k)
                        if j < 16:
                            kt = 2 * (j % 8) + k
                            if first and j < 8:
                                pe.wait_ge(h2_lo_ready, kt + 1)
                            last = feature_major((SET_P, SET_Q)[j // 8], w, h_hi, h_lo, kt, KT)
                        else:
                            g, v = divmod(j - 16, 4)
                            pe.wait_ge(u_lo_ready, ck * 8 + (2 * v + k + 1))
                            last = token_major((SET_P, SET_Q)[g % 2], w, u_hi, u_lo, 2 * v + k, FT)
                    last.then_inc(unit_used, 1)
                    if first and j in GATE2_AFTER:
                        q = GATE2_AFTER.index(j)
                        if q < 2:
                            pe.wait_ge(relu_done, 4 * (q + 1))
                        else:
                            pe.wait_ge(y2_done, 4 * (q - 1))
                        row_job(20 + q, banks[4 * (q % 2)])

            chunk(0, first=True)
            with pe.Fori(1, CHUNKS - 1) as ck:
                chunk(ck)
            ck = CHUNKS - 1
            chunk(ck, last_chunk=True)
            pe.wait_ge(y2_done, ck * 16 + 8)
            for t in range(NT):
                for v in range(4):
                    j = PER_CHUNK - 4 + v
                    pe.wait_ge(lo_ready, ck * PER_CHUNK + (U_MLP + j - 7))
                    for k in range(2):
                        last = token_major(SET_Q, w_tile((U_MLP + j) % RING, k), u_hi, u_lo, 2 * v + k, FT, [t])
                last.then_inc(out_tile, 1)

        @block.scalar
        def _(act):
            steps = [0]

            def step(ins):
                ins.then_inc(act_step, 1)
                steps[0] += 1
                act.wait_ge(act_step, steps[0])

            def hi_part(n):
                slot, count, s = unit(n)
                act.wait_ge(raw_in[slot], count)
                if n >= RING:
                    act.wait_ge(unit_used, n - RING + 1)
                act.activation(w_hi[:, s], raw[:, slot], ACT.Copy).then_inc(hi_ready, 1)

            act.dma_start(cc[:, 0, :], c.rearrange("b (p k) -> (b p) k", p=P)).then_inc(c_in, 16)
            act.wait_ge(c_in, 16)
            act.activation(cc[:, 1, :], cc[:, 0, :], ACT.Exp, scale=-1.0).then_inc(c_exp, 1)
            def row_rms(t):
                act.wait_ge(x_in[t], 16)
                if t:
                    act.wait_ge(x_ssq, t)
                act.activation(junk[:, :], x_tok[:, t], ACT.Square, accum_out=stat[:, XS + t:XS + t + 1]).then_inc(x_ssq, 1)
                act.wait_ge(x_ssq, t + 1)
                act.activation(stat[:, XR + t:XR + t + 1], stat[:, XS + t:XS + t + 1], ACT.Sqrt, bias=eps[:, :],
                               scale=1.0 / D).then_inc(x_std, 1)

            def copy_turned(t):
                for g in range(4):
                    act.wait_ge(xt_done, 4 * t + g + 1)
                    act.activation(xnT[:, 4 * g:4 * g + 4, t * P:(t + 1) * P],
                                   banks[4 * (t % 2) + g][:, :].rearrange("p (k n) -> p k n", n=P), ACT.Copy).then_inc(xt_copied, 1)

            act.wait_ge(const_ready, 3)
            row_rms(0)
            row_rms(1)
            for t in range(2, NT):
                row_rms(t)
                copy_turned(t - 2)
            copy_turned(NT - 2)
            copy_turned(NT - 1)
            act.wait_ge(vec_turned, 1)
            act.activation(vcol[:, :], banks[7][:, 0:112], ACT.Copy).then_inc(vcol_ready, 1)
            act.wait_ge(vcol_ready, 1)
            step(act.activation(lam[:, 0, :], col(LAMBDA, 0, CT), ACT.Abs))
            act.activation(lam[:, 1, :], lam[:, 0, :], ACT.Exp, scale=-1.0).then_inc(lam_exp, 1)

            act.wait_ge(gw_zero, 2)
            for w, dst in ((w_rg, wrg), (w_ig, wig)):
                for b in range(2):
                    act.dma_start(dst[b * LB:(b + 1) * LB, :, b * LB:(b + 1) * LB],
                                  w[0, b:2 * CT:2].rearrange("n i j -> i n j")).then_inc(gw_in, 16)

            act.wait_ge(xt_copied, KT)
            for j in range(8):
                hi_part(2 * j)
                hi_part(2 * j + 1)
                act.wait_ge(mod_read, j + 1)
                for kt in (2 * j, 2 * j + 1):
                    act.activation(h_hi[:, kt, :], xnT[:, kt, :], ACT.Identity, bias=S1[:, kt:kt + 1],
                                   scale=A1[:, kt:kt + 1]).then_inc(h_hi_ready, 1)

            def copy_u(ch):
                act.activation(ut[:, ch, :], banks[ch][:, :], ACT.Copy).then_inc(u_copied, 1)

            def sigmoids(ch):
                act.wait_ge(z_done, ch + 1)
                b = 4 + 2 * (ch % 2)
                act.activation(rg[:, ch, :], banks[b][:, :], ACT.Sigmoid, bias=col(B_RG, ch)).then_inc(sig_done, 1)
                act.activation(ig[:, ch, :], banks[b + 1][:, :], ACT.Sigmoid, bias=col(B_IG, ch)).then_inc(sig_done, 1)

            def decay(ch):
                act.wait_ge(kp_ready, 1)
                act.wait_ge(sig_done, 2 * ch + 1)
                act.activation(ut[:, ch, :], rg[:, ch, :], ACT.Tanh, scale=lam[:, 6, ch:ch + 1])
                step(act.activation(rg[:, ch, :], rg[:, ch, :], ACT.Exp, scale=lam[:, 7, ch:ch + 1]))
                if ch >= 2:
                    act.wait_ge(m_ready, ch - 1)
                act.activation(a_sq[:, ch % 2, :], rg[:, ch, :], ACT.Square).then_inc(decay_ready, 1)

            def root(ch):
                act.wait_ge(m_ready, ch + 1)
                act.activation(ut[:, ch, :], ut[:, ch, :], ACT.Sqrt).then_inc(root_ready, 1)

            def gelu(ch):
                act.wait_ge(unit_used, U_PROJ + (8 if ch < 4 else 16))
                act.wait_ge(bx_ready, ch + 1)
                act.activation(ut[:, ch, :], banks[ch][:, :], ACT.Gelu_apprx_tanh).then_inc(gelu_done, 1)

            def exps(h):
                for e, i in enumerate((1, 0, 2, 3)):
                    act.wait_ge(neg_max, 4 * h + e + 1)
                    n_keys = (i + 1) * P
                    act.activation(LP[:, LP_AT[i]:LP_AT[i] + n_keys], LP[:, LP_AT[i]:LP_AT[i] + n_keys], ACT.Exp,
                                   bias=stat[:, NM + i:NM + i + 1], accum_out=stat[:, ES + i:ES + i + 1]).then_inc(exp_done, 1)

            for n in range(U_LAST, U_ATT + LAG):
                hi_part(n)
                if n == U_ATT:
                    act.wait_ge(unit_used, U_ATT - 4)
                    for ch in range(CT):
                        act.activation(yl_hi[:, ch, :], hs[:, ch, :], ACT.Copy, scale=col(G_LRU, ch)).then_inc(yl_hi_ready, 1)
                    exps(0)
                done = n - LAG + 1
                if done == U_LAST:
                    act.wait_ge(unit_used, U_LAST)
                    for ch in range(CT - 1):
                        copy_u(ch)
                if done == U_PROJ:
                    act.wait_ge(unit_used, U_PROJ)
                    copy_u(CT - 1)
                e = n - U_PROJ
                for ch in {3: [0], 4: [1], 5: [2], 6: [3], 8: [4, 5], 10: [6, 7]}.get(e, []):
                    sigmoids(ch)
                for ch in {7: [0, 1, 2, 3], 11: [4, 5], 12: [6, 7]}.get(e, []):
                    decay(ch)
                if e == 13:
                    for ch in range(CT):
                        root(ch)
                if e == 14:
                    for ch in range(4):
                        gelu(ch)
                if e == 18:
                    for ch in range(4, 8):
                        gelu(ch)
                if e == 30:
                    act.wait_ge(wf_in, 16)
                    act.wait_ge(wf_zero, 2)
                    act.activation(wf_hi[:, :, 0:HEADS], wf_raw[:, :, :], ACT.Copy).then_inc(wf_hi_ready, 1)
                for gi, dst, done_sem in ((2, qT, q_copied), (3, qT, q_copied), (4, kT, k_copied), (5, kT, k_copied)):
                    if done == U_PROJ + 8 * (gi + 1):
                        act.wait_ge(unit_used, done)
                        if gi == 2:
                            act.wait_ge(scan_done, CT)
                        if gi == 4:
                            act.wait_ge(scan_done, CT)
                        for m in range(4):
                            act.activation(dst[:, 4 * (gi % 2) + m, :], banks[4 * (gi % 2) + m][:, :], ACT.Copy,
                                           scale=DH ** -0.5 if dst is qT else 1.0).then_inc(done_sem, 1)
                if e == 6 * 8 + 3:
                    act.wait_ge(f_done, 1)
                    act.wait_ge(bf_in, 16)
                    act.wait_ge(ssq_done, CT)
                    act.activation(ut[0:HEADS, 0, :], banks[0][0:HEADS, :], ACT.Identity, bias=bf[:, :]).then_inc(f_read, 1)
                    act.wait_ge(f_read, 1)
                    step(act.activation(ut[0:HEADS, 1, :], ut[0:HEADS, 0, :], ACT.Abs))
                    act.activation(ut[0:HEADS, 2, :], ut[0:HEADS, 1, :], ACT.Exp, scale=-1.0).then_inc(f_exp, 1)
                if e == 7 * 8 + 1:
                    act.wait_ge(row_done, 1)
                    act.activation(stat[:, RL:RL + NT], banks[2][:, 0:NT], ACT.Sqrt, bias=eps[:, :], scale=1.0 / D_LRU).then_inc(row_std, 1)
                for gi in (6, 7):
                    if done == U_PROJ + 8 * (gi + 1):
                        act.wait_ge(unit_used, done)
                        act.wait_ge(nf_stored, 16)
                        for t in range(NT):
                            act.activation(vv[:, t, (gi - 6) * COLS:(gi - 5) * COLS], banks[(4, 0)[gi - 6] + t][:, :],
                                           ACT.Copy).then_inc(v_copied, 1)

            def copy_pt(h):
                if h:
                    act.wait_ge(pv_done, h)
                for e, (b, c0, width, dst) in enumerate(((banks[6], 0, 2 * P, PT_AT[2]), (banks[5], 0, 4 * P, PT_AT[1]),
                                                         (banks[4], 0, 4 * P, PT_AT[0]))):
                    act.wait_ge(pt_done, 3 * h + e + 1)
                    act.activation(PT[:, dst:dst + width], b[:, c0:c0 + width], ACT.Copy).then_inc(pt_copied, 1)

            def head_out(h):
                act.wait_ge(pv_done, h + 1)
                if h:
                    act.wait_ge(att_ssq, h)
                act.activation(g_row[:, :], banks[7][:, :], ACT.Square).then_inc(ya_sq, 1)
                act.activation(ya_hi[:, h, :], banks[7][:, :], ACT.Copy, scale=col(G_ATT, h)).then_inc(ya_hi_ready, 1)

            def copy_half(bank_of, dst):
                for t in range(NT):
                    act.activation(dst(t), bank_of[t][:, :], ACT.Copy, scale=stat[:, RL + t:RL + t + 1]).then_inc(half_copied, 1)

            act.wait_ge(row_ready, 1)
            for h in range(HEADS):
                if h:
                    exps(h)
                    head_out(h - 1)
                hi_part(U_ATT + LAG + h)
                copy_pt(h)
                if h % 4 == 3:
                    act.wait_ge(unit_used, U_ATT + h + 1)
                    if h == 3:
                        act.wait_ge(yl_lo_ready, CT)
                    copy_half(SET_P, lambda t: yacc[:, t, h // 4, :])
            head_out(HEADS - 1)

            def square_y(r, t):
                g, e = REST[r][0], 4 * [1, 2, 3, 5].index(r) + t
                act.wait_ge(y_sum, e + 1)
                if e:
                    act.wait_ge(y_sq, e)
                act.activation(junk2[:, 0:COLS], yg[:, t, g * COLS:(g + 1) * COLS], ACT.Square,
                               accum_out=stat[:, YS + 4 * t + g:YS + 4 * t + g + 1]).then_inc(y_sq, 1)

            def mix_evacuation(r):
                g, half = REST[r]
                cols = slice(g * COLS, (g + 1) * COLS)
                if half == 0:
                    act.wait_ge(unit_used, U_OUT + 4 * r + 4)
                    copy_half(SET_P, lambda t: yg[:, t, cols])
                else:
                    for t in range(NT):
                        square_y(r, t)

            for n in range(U_OUT + LAG, U_MLP):
                hi_part(n)
                done = n - LAG + 1 - U_OUT
                if done == 3:
                    act.wait_ge(row_done, 2)
                    act.activation(stat[:, RA:RA + NT], banks[4][:, 0:NT], ACT.Sqrt, bias=eps[:, :], scale=1.0 / D_ATT).then_inc(row_std, 1)
                if done and done % 4 == 0:
                    mix_evacuation(done // 4 - 1)

            def mix_rms(t):
                square_y(len(REST) - 1, t)
                act.wait_ge(mix_sum, t + 1)
                act.activation(stat[:, YR + t:YR + t + 1], stat[:, YR + t:YR + t + 1], ACT.Sqrt, bias=eps[:, :],
                               scale=1.0 / D).then_inc(mix_std, 1)

            def x1_rms(t):
                act.wait_ge(x1_done, t + 1)
                act.wait_ge(y_sq, 12 + t + 1)
                if t:
                    act.wait_ge(x1_ssq, t)
                act.activation(junk2[:, :], yg[:, t, :], ACT.Square, accum_out=stat[:, X1S + t:X1S + t + 1]).then_inc(x1_ssq, 1)
                act.wait_ge(x1_ssq, t + 1)
                act.activation(stat[:, X1S + t:X1S + t + 1], stat[:, X1S + t:X1S + t + 1], ACT.Sqrt, bias=eps[:, :],
                               scale=1.0 / D).then_inc(x1_std, 1)

            def copy_turned_x1(t):
                for g in range(4):
                    act.wait_ge(x1t_done, 4 * t + g + 1)
                    act.activation(x1T[:, 4 * g:4 * g + 4, t * P:(t + 1) * P],
                                   (SET_P, SET_Q)[t % 2][g][:, :].rearrange("p (k n) -> p k n", n=P), ACT.Copy).then_inc(x1t_copied, 1)

            def modulate(kt):
                act.wait_ge(x1t_copied, 4 * (NT - 1) + kt // 4 + 1)
                act.activation(h_hi[:, kt, :], x1T[:, kt, :], ACT.Identity, bias=S2[:, kt:kt + 1],
                               scale=A2[:, kt:kt + 1]).then_inc(h2_hi_ready, 1)

            for t in range(NT):
                mix_rms(t)
                if t == NT - 2:
                    hi_part(U_MLP)
                if t == NT - 1:
                    copy_turned_x1(0)
                x1_rms(t)
            hi_part(U_MLP + 1)
            copy_turned_x1(1)
            hi_part(U_MLP + 2)
            copy_turned_x1(2)
            copy_turned_x1(3)

            def hidden(ck, g):
                for m in range(4):
                    e = 4 * g + m
                    act.wait_ge(unit_used, ck * PER_CHUNK + (U_MLP + 8 * (g + 1)))
                    if e >= 2 or not (isinstance(ck, int) and ck == 0):
                        act.wait_ge(u_sq, ck * 8 + (e - 1))
                    act.activation(rt[:, m % 2, :], (SET_P, SET_Q)[g][m][:, :], ACT.Relu).then_inc(relu_done, 1)
                    act.wait_ge(relu_done, ck * 8 + (e + 1))
                    act.activation(u_hi[:, e, :], rt[:, m % 2, :], ACT.Square).then_inc(u_hi_ready, 1)

            def hi_of_chunk(ck, j):
                slot, count = chunk_raw(ck, j)
                act.wait_ge(raw_in[slot], count)
                act.wait_ge(unit_used, ck * PER_CHUNK + (U_MLP + j - RING + 1))
                act.activation(w_hi[:, (U_MLP + j) % RING], raw[:, slot], ACT.Copy).then_inc(hi_ready, 1)

            def chunk(ck, j0=0, last=False):
                for j in range(j0, PER_CHUNK):
                    hi_of_chunk(ck, j)
                    if j == 7 + LAG:
                        hidden(ck, 0)
                    if j == 15 + LAG:
                        hidden(ck, 1)
                    if last and j in (19 + LAG, 23 + LAG):
                        final_squares((j - 19 - LAG) // 4)

            def final_square(g, t):
                act.wait_ge(y2_done, 16 * (CHUNKS - 1) + 4 * g + t + 1)
                if g or t:
                    act.wait_ge(f_ssq, 4 * g + t)
                act.activation(junk3[:, :], y2[:, t, g * COLS:(g + 1) * COLS], ACT.Square,
                               accum_out=stat[:, FS + 4 * t + g:FS + 4 * t + g + 1]).then_inc(f_ssq, 1)

            def final_squares(g):
                for t in range(NT):
                    final_square(g, t)

            for kt in range(KT):
                modulate(kt)
                if kt >= 3 and kt % 2:
                    hi_of_chunk(0, LAG + (kt - 3) // 2)
            chunk(0, LAG + 7)
            with act.Fori(1, CHUNKS - 1) as ck:
                chunk(ck)
            chunk(CHUNKS - 1, last=True)
            final_squares(2)
            for t in range(NT):
                final_square(3, t)
                act.wait_ge(fin_sum, t + 1)
                act.activation(stat[:, FR + t:FR + t + 1], stat[:, FR + t:FR + t + 1], ACT.Sqrt, bias=eps[:, :],
                               scale=1.0 / D).then_inc(fin_std, 1)

        @block.vector
        def _(dve):
            steps = [0]

            def step(ins):
                ins.then_inc(dve_step, 1)
                steps[0] += 1
                dve.wait_ge(dve_step, steps[0])

            def lo_part(n):
                slot, _, s = unit(n)
                dve.wait_ge(hi_ready, n + 1)
                dve.tensor_tensor(w_lo[:, s], raw[:, slot], w_hi[:, s].bitcast(F32), ALU.subtract).then_inc(lo_ready, 1)

            def log1p_part(e, d, s, s2, q):
                step(dve.tensor_scalar(d, e, 2.0, None, ALU.add))
                step(dve.reciprocal(d, d))
                step(dve.tensor_tensor(s, e, d, ALU.mult))
                step(dve.tensor_tensor(s2, s, s, ALU.mult))
                step(dve.tensor_scalar(q, s2, 1.0 / 17, None, ALU.mult))
                for k in range(7, 0, -1):
                    step(dve.scalar_tensor_tensor(q, q, 1.0 / (2 * k + 1), s2, ALU.add, ALU.mult))
                step(dve.scalar_tensor_tensor(q, q, 1.0, s, ALU.add, ALU.mult))

            dve.wait_ge(c_exp, 1)
            step(dve.tensor_scalar(cc[:, 1, :], cc[:, 1, :], 1.0, None, ALU.add))
            step(dve.reciprocal(cc[:, 1, :], cc[:, 1, :]))
            step(dve.tensor_tensor(cc[:, 2, :], cc[:, 0, :], cc[:, 1, :], ALU.mult))

            def weigh_rows(m, k0, rows, used, count):
                a = acc[:, m % 2, :]
                for r, row in enumerate(rows):
                    k = k0 + r
                    if k == 0:
                        dve.wait_ge(init_in, 32 * (m + 1) if m < 8 else 16 * (m + 9))
                        if m >= 2:
                            dve.wait_ge(acc_read, m - 1)
                    ins = dve.scalar_tensor_tensor(a, row, cc[:, 2, k:k + 1], a if k else acc_init[:, :], ALU.mult, ALU.add)
                    if k == 0:
                        ins.then_inc(acc_first, 1)
                        dve.wait_ge(acc_first, m + 1)
                    elif r == len(rows) - 1:
                        ins.then_inc(used, 1)
                        dve.wait_ge(used, count)
                    else:
                        step(ins)

            def start_sums(j, q):
                dve.wait_ge(gst_in[q], 32 * (j + 1))
                weigh_rows(j, 4 * q, [gst[q][:, r].rearrange("p a b -> p (a b)") for r in range(4)], gst_used, 4 * j + q + 1)

            def ada_unit(a):
                cg, r = divmod(a, 8)
                slot, count = place(ada_pos[a])
                dve.wait_ge(raw_in[slot], count)
                weigh_rows(8 + cg, 2 * r, [raw[:, slot, 0:COLS], raw[:, slot, COLS:]], ada_used, a + 1)

            def take_start(j):
                dve.wait_ge(acc_read, j + 1)
                step(dve.scalar_tensor_tensor(A1[:, 2 * j:2 * j + 2], banks[7][:, 0:2], 1.0, col(G_PRE_MIX, 2 * j, 2), ALU.add, ALU.mult))
                dve.tensor_copy(S1[:, 2 * j:2 * j + 2], banks[7][:, 2:4]).then_inc(mod_read, 1)

            def take_columns(cg, bank):
                dve.wait_ge(acc_read, 8 + cg + 1)
                by_block = bank[:, :].rearrange("p (b n) -> p b n", n=P)
                if cg < 4:
                    step(dve.tensor_reduce(mod[:, :], by_block, AX, ALU.add))
                    dve.scalar_tensor_tensor(A2[:, 4 * cg:4 * cg + 4], mod[:, :], 1.0, col(G_PRE_MLP, 4 * cg, 4),
                                             ALU.add, ALU.mult).then_inc(mod_read, 1)
                else:
                    dve.tensor_reduce(S2[:, 4 * cg - 16:4 * cg - 12], by_block, AX, ALU.add).then_inc(mod_read, 1)
                dve.wait_ge(mod_read, 8 + cg + 1)

            def take_gate(q, bank):
                dve.wait_ge(acc_read, 17 + q)
                dve.wait_ge(gain_in, 16 * (q + 1))
                dst = (G1, G2)[q // 4][:, q % 4 * COLS:(q % 4 + 1) * COLS]
                dve.tensor_tensor(dst, bank[:, :], g_row[:, :], ALU.mult).then_inc(gate_ready, 1)

            for t in range(NT):
                dve.wait_ge(x_std, t + 1)
                step(dve.reciprocal(stat[:, XR + t:XR + t + 1], stat[:, XR + t:XR + t + 1]))
                dve.tensor_scalar(x_tok[:, t, :], x_tok[:, t, :], stat[:, XR + t:XR + t + 1], None, ALU.mult).then_inc(x_scaled, 1)
            dve.wait_ge(const_ready, 4)
            for j in range(8):
                start_sums(j, 0)
                if j:
                    take_start(j - 1)
                for q in range(1, 4):
                    start_sums(j, q)
                lo_part(2 * j)
            take_start(7)

            dve.wait_ge(lam_exp, 1)
            log1p_part(lam[:, 1, :], lam[:, 2, :], lam[:, 3, :], lam[:, 4, :], lam[:, 5, :])
            step(dve.tensor_scalar(lam[:, 2, :], col(LAMBDA, 0, CT), -1.0, 0.0, ALU.mult, ALU.max))
            step(dve.scalar_tensor_tensor(lam[:, 3, :], lam[:, 5, :], 2.0, lam[:, 2, :], ALU.mult, ALU.add))
            step(dve.tensor_scalar(lam[:, 6, :], lam[:, 3, :], LRU_C, None, ALU.mult))
            dve.tensor_scalar(lam[:, 7, :], lam[:, 3, :], -LRU_C, None, ALU.mult).then_inc(kp_ready, 1)

            def conv(ch):
                dve.wait_ge(u_copied, ch + 1)
                o = hs[:, ch, :]
                step(dve.tensor_scalar(o, ut[:, ch, :], col(CONVW, 8 * (CW - 1) + ch), col(CONVB, ch), ALU.mult, ALU.add))
                for d in range(1, CW):
                    ins = dve.scalar_tensor_tensor(o[:, d:], ut[:, ch, 0:S - d], col(CONVW, 8 * (CW - 1 - d) + ch), o[:, d:],
                                                   ALU.mult, ALU.add)
                    if d < CW - 1:
                        step(ins)
                    else:
                        ins.then_inc(conv_done, 1)

            def one_minus_square(ch):
                dve.wait_ge(decay_ready, ch + 1)
                dve.scalar_tensor_tensor(ut[:, ch, :], a_sq[:, ch % 2, :], 1.0, ut[:, ch, :], ALU.add, ALU.mult).then_inc(m_ready, 1)

            def recurrence(ch):
                dve.wait_ge(root_ready, ch + 1)
                dve.wait_ge(ix_ready, ch + 1)
                dve.tensor_tensor(ig[:, ch, :], ut[:, ch, :], ig[:, ch, :], ALU.mult).then_inc(bx_ready, 1)
                dve.wait_ge(bx_ready, ch + 1)
                dve.tensor_tensor_scan(hs[:, ch, :], rg[:, ch, :], ig[:, ch, :], 0.0, ALU.mult, ALU.add).then_inc(scan_done, 1)

            def gate(ch):
                dve.wait_ge(gelu_done, ch + 1)
                dve.wait_ge(scan_done, ch + 1)
                dve.tensor_tensor(hs[:, ch, :], hs[:, ch, :], ut[:, ch, :], ALU.mult).then_inc(y_done, 1)

            def forget():
                dve.wait_ge(f_exp, 1)
                t = lambda i: ut[0:HEADS, i, :]
                log1p_part(t(2), t(3), t(4), t(5), t(6))
                step(dve.tensor_scalar(t(3), t(0), -1.0, 0.0, ALU.mult, ALU.max))
                step(dve.scalar_tensor_tensor(t(4), t(6), 2.0, t(3), ALU.mult, ALU.add))
                step(dve.memset(t(5), 1.0))
                dve.tensor_tensor_scan(t(7), t(5), t(4), 0.0, ALU.mult, ALU.add).then_inc(nf_ready, 1)

            def lru_low(ch):
                dve.wait_ge(yl_hi_ready, ch + 1)
                dve.wait_ge(unit_used, U_ATT - 3 + ch // 2)
                dve.scalar_tensor_tensor(yl_lo[:, ch, :], hs[:, ch, :], col(G_LRU, ch), yl_hi[:, ch, :].bitcast(F32),
                                         ALU.mult, ALU.subtract).then_inc(yl_lo_ready, 1)

            def softmax_rows(h):
                dve.wait_ge(nf_in[h % 2], 16 * (h // 2 + 1))
                dve.wait_ge(nfm_ready, h + 1)
                for e, i in enumerate((1, 0, 2, 3)):
                    if i != 0:
                        dve.wait_ge(score_done, 3 * h + {1: 1, 2: 2, 3: 3}[i])
                    else:
                        dve.wait_ge(score_done, 3 * h + 2)
                    b, c0 = SCORE_AT[i]
                    L = LP[:, LP_AT[i]:LP_AT[i] + (i + 1) * P]
                    nF0 = nF[:, h % 2, i * P:i * P + 1]
                    if i:
                        dve.scalar_tensor_tensor(L[:, 0:i * P], nF[:, h % 2, 0:i * P], nF0, b[:, c0:c0 + i * P], ALU.subtract, ALU.add)
                    step(dve.scalar_tensor_tensor(L[:, i * P:], nFm[:, i * P:(i + 1) * P], nF0, b[:, c0 + i * P:c0 + (i + 1) * P],
                                                  ALU.subtract, ALU.add))
                    dve.tensor_reduce(stat[:, NM + i:NM + i + 1], L, AX, ALU.max, negate=True).then_inc(neg_max, 1)
                dve.wait_ge(exp_done, 4 * (h + 1))
                step(dve.reciprocal(stat[:, ES:ES + NT], stat[:, ES:ES + NT]))
                for i in range(NT):
                    L = LP[:, LP_AT[i]:LP_AT[i] + (i + 1) * P]
                    dve.tensor_scalar(L, L, stat[:, ES + i:ES + i + 1], None, ALU.mult).then_inc(prob_ready, 1)

            for n in range(U_LAST, U_ATT + LAG):
                lo_part(n)
                for a in ada_of[n]:
                    ada_unit(a)
                if n == U_ATT:
                    softmax_rows(0)
                for ch in {U_ATT + 1: range(4), U_ATT + 2: range(4, CT)}.get(n, ()):
                    lru_low(ch)
                e = n - U_PROJ
                if 0 <= e < CT:
                    conv(e)
                for ch in {7: [0, 1, 2, 3], 12: [4, 5, 6, 7]}.get(e, []):
                    one_minus_square(ch)
                if e in (14, 15):
                    for ch in range(4 * (e - 14), 4 * (e - 13)):
                        recurrence(ch)
                if e == 18:
                    for ch in range(4):
                        gate(ch)
                if e == 20:
                    for ch in range(4, 8):
                        gate(ch)
                if e == 31:
                    dve.wait_ge(wf_hi_ready, 1)
                    dve.tensor_tensor(wf_lo[:, :, 0:HEADS], wf_raw[:, :, :], wf_hi[:, :, 0:HEADS].bitcast(F32),
                                      ALU.subtract).then_inc(wf_lo_ready, 1)
                if e == 6 * 8 + 3:
                    forget()
                for gi in range(1, 8):
                    if e == 8 * gi + COLUMNS_AT[gi] + LAG:
                        take_columns(gi - 1, (banks[1] if gi == 6 else banks[5]) if gi >= 6 else banks[(4, 0)[gi % 2]])
                if e == 7 * 8 + 2:
                    dve.wait_ge(row_std, 1)
                    dve.reciprocal(stat[:, RL:RL + NT], stat[:, RL:RL + NT]).then_inc(row_ready, 1)
                if e == 7 * 8 + 6 + LAG:
                    take_columns(7, banks[7])

            def head_low(h):
                dve.wait_ge(ya_hi_ready, h + 1)
                dve.scalar_tensor_tensor(ya_lo[:, h, :], banks[7][:, :], col(G_ATT, h), ya_hi[:, h, :].bitcast(F32),
                                         ALU.mult, ALU.subtract).then_inc(ya_lo_ready, 1)

            for h in range(HEADS):
                if h:
                    softmax_rows(h)
                    head_low(h - 1)
                lo_part(U_ATT + LAG + h)
                for a in ada_of[U_ATT + LAG + h]:
                    ada_unit(a)
            head_low(HEADS - 1)

            def sum_y(r, t):
                g = REST[r][0]
                cols = slice(g * COLS, (g + 1) * COLS)
                dve.scalar_tensor_tensor(yg[:, t, cols], (SET_P, SET_Q)[r % 2][t][:, :], stat[:, RA + t:RA + t + 1],
                                         yacc[:, t, g, :] if g < 2 else yg[:, t, cols], ALU.mult, ALU.add).then_inc(y_sum, 1)

            def gate_y(r, t):
                g = REST[r][0]
                cols = slice(g * COLS, (g + 1) * COLS)
                dve.wait_ge(y_sq, 4 * [1, 2, 3, 5].index(r) + t + 1)
                dve.tensor_tensor(yg[:, t, cols], yg[:, t, cols], G1[:, cols], ALU.mult).then_inc(y_gated, 1)

            for n in range(U_OUT + LAG, U_MLP):
                lo_part(n)
                for a in ada_of[n]:
                    ada_unit(a)
                done = n - LAG + 1 - U_OUT
                if done == 3:
                    take_gate(0, banks[5])
                    dve.wait_ge(row_std, 2)
                    step(dve.reciprocal(stat[:, RA:RA + NT], stat[:, RA:RA + NT]))
                for q, at in ((1, 7), (2, 15), (3, 19)):
                    if done == at:
                        take_gate(q, SET_P[0] if q < 3 else SET_Q[0])
                r = done // 4 - 1
                if r >= 1 and REST[r][1]:
                    if done % 4 == 0:
                        dve.wait_ge(unit_used, U_OUT + 4 * r + 4)
                        dve.wait_ge(half_copied, {0: 4, 1: 8, 2: 12}[REST[r][0]])
                        for t in range(NT):
                            sum_y(r, t)
                    elif done % 4 == 1:
                        for t in range(NT):
                            gate_y(r, t)

            last = len(REST) - 1
            dve.wait_ge(half_copied, 16)
            def x1_diagonal(t):
                dve.wait_ge(x1_std, t + 1)
                step(dve.reciprocal(stat[:, X1R_ + t:X1R_ + t + 1], stat[:, X1S + t:X1S + t + 1]))
                dve.tensor_scalar(x1diag[:, t, :], ident[:, :], stat[:, X1R_ + t:X1R_ + t + 1], None, ALU.mult).then_inc(x1diag_ready, 1)

            for t in range(NT):
                dve.wait_ge(mix_tile, t + 1) if t < NT - 1 else dve.wait_ge(unit_used, U_MLP)
                sum_y(last, t)
                if t:
                    x1_diagonal(t - 1)
                gate_y(last, t)
                dve.tensor_reduce(stat[:, YR + t:YR + t + 1], stat[:, YS + 4 * t:YS + 4 * t + 4], AX, ALU.add).then_inc(mix_sum, 1)
                dve.wait_ge(mix_std, t + 1)
                step(dve.reciprocal(stat[:, YR + t:YR + t + 1], stat[:, YR + t:YR + t + 1]))
                dve.wait_ge(xr_in[t], 16)
                dve.wait_ge(y_gated, 12 + t + 1)
                src = xr2[:, :] if t == 2 else xr[:, t % 2, :]
                dve.scalar_tensor_tensor(yg[:, t, :], yg[:, t, :], stat[:, YR + t:YR + t + 1], src, ALU.mult, ALU.add).then_inc(x1_done, 1)
            lo_part(U_MLP)
            x1_diagonal(NT - 1)
            lo_part(U_MLP + 1)
            lo_part(U_MLP + 2)

            def modulate(kt):
                dve.wait_ge(h2_hi_ready, kt + 1)
                h = x1T[:, kt, :]
                dve.tensor_scalar(h, h, A2[:, kt:kt + 1], S2[:, kt:kt + 1], ALU.mult, ALU.add).then_inc(h2_sum, 1)
                dve.wait_ge(h2_sum, kt + 1)
                dve.tensor_tensor(h_lo[:, kt, :], h, h_hi[:, kt, :].bitcast(F32), ALU.subtract).then_inc(h2_lo_ready, 1)

            def lo_of_chunk(ck, j):
                slot, _ = chunk_raw(ck, j)
                s = (U_MLP + j) % RING
                dve.wait_ge(hi_ready, ck * PER_CHUNK + (U_MLP + j + 1))
                dve.tensor_tensor(w_lo[:, s], raw[:, slot], w_hi[:, s].bitcast(F32), ALU.subtract).then_inc(lo_ready, 1)

            def hidden(ck, g):
                for m in range(4):
                    e = 4 * g + m
                    dve.wait_ge(relu_done, ck * 8 + (e + 1))
                    if e or not (isinstance(ck, int) and ck == 0):
                        dve.wait_ge(u_lo_ready, ck * 8 + e)
                    dve.tensor_tensor(u_full_t[:, :], rt[:, m % 2, :], rt[:, m % 2, :], ALU.mult).then_inc(u_sq, 1)
                    dve.wait_ge(u_sq, ck * 8 + (e + 1))
                    dve.wait_ge(u_hi_ready, ck * 8 + (e + 1))
                    dve.tensor_tensor(u_lo[:, e, :], u_full_t[:, :], u_hi[:, e, :].bitcast(F32), ALU.subtract).then_inc(u_lo_ready, 1)

            def add_out(ck, g, j_end, first=False):
                bank_of = (SET_P, SET_Q)[g % 2]
                cols = slice(g * COLS, (g + 1) * COLS)
                dve.wait_ge(unit_used, ck * PER_CHUNK + (U_MLP + j_end))
                if first:
                    dve.wait_ge(x1_stored, 16 * NT)
                else:
                    dve.wait_ge(y2_done, ck * 16 + 4 * g)
                for t in range(NT):
                    if first:
                        dve.tensor_copy(y2[:, t, cols], bank_of[t][:, :]).then_inc(y2_done, 1)
                    else:
                        dve.tensor_tensor(y2[:, t, cols], bank_of[t][:, :], y2[:, t, cols], ALU.add).then_inc(y2_done, 1)

            def gate_out(g, t):
                dve.wait_ge(f_ssq, 4 * g + t + 1)
                cols = slice(g * COLS, (g + 1) * COLS)
                dve.tensor_tensor(y2[:, t, cols], y2[:, t, cols], G2[:, cols], ALU.mult).then_inc(y2_gated, 1)

            def chunk(ck, j0=LAG, first=False, last=False):
                for j in range(j0, PER_CHUNK):
                    lo_of_chunk(ck, j)
                    if first:
                        for a in ada_of[U_MLP + j]:
                            ada_unit(a)
                    if j == 7 + LAG:
                        hidden(ck, 0)
                    if j == 15 + LAG:
                        hidden(ck, 1)
                    if j in (19 + LAG, 23 + LAG, 27 + LAG):
                        add_out(ck, (j - 19 - LAG) // 4, j - LAG + 1, first)
                    if first and j - LAG in GATE2_AFTER:
                        q = GATE2_AFTER.index(j - LAG)
                        take_gate(4 + q, banks[4 * (q % 2)])
                    if last and j in (20 + LAG, 24 + LAG, 28 + LAG):
                        for t in range(NT):
                            gate_out((j - 20 - LAG) // 4, t)

            def next_units(ck):
                for j in range(LAG):
                    lo_of_chunk(ck + 1, j)
                add_out(ck, 3, PER_CHUNK, isinstance(ck, int) and ck == 0)

            for kt in range(KT):
                modulate(kt)
                if kt >= 3 and kt % 2:
                    lo_of_chunk(0, LAG + (kt - 3) // 2)
                    for a in ada_of[U_MLP + LAG + (kt - 3) // 2]:
                        ada_unit(a)
            chunk(0, LAG + 7, first=True)
            next_units(0)
            with dve.Fori(1, CHUNKS - 1) as ck:
                chunk(ck)
                next_units(ck)
            chunk(CHUNKS - 1, last=True)
            g = 3
            cols = slice(g * COLS, (g + 1) * COLS)
            dve.wait_ge(y2_done, (CHUNKS - 1) * 16 + 4 * g)
            for t in range(NT):
                dve.wait_ge(out_tile, t + 1)
                dve.tensor_tensor(y2[:, t, cols], SET_Q[t][:, :], y2[:, t, cols], ALU.add).then_inc(y2_done, 1)
                gate_out(g, t)
                dve.tensor_reduce(stat[:, FR + t:FR + t + 1], stat[:, FS + 4 * t:FS + 4 * t + 4], AX, ALU.add).then_inc(fin_sum, 1)
                dve.wait_ge(fin_std, t + 1)
                step(dve.reciprocal(stat[:, FR + t:FR + t + 1], stat[:, FR + t:FR + t + 1]))
                dve.wait_ge(y2_gated, 4 * g + t + 1)
                dve.wait_ge(x1r_in, 16 * NT)
                for half in range(2):
                    h = slice(half * (D // 2), (half + 1) * (D // 2))
                    dve.scalar_tensor_tensor(x1r[:, t, h], y2[:, t, h], stat[:, FR + t:FR + t + 1], x1r[:, t, h],
                                             ALU.mult, ALU.add).then_inc(out_ready, 1)

        @block.gpsimd
        def _(pool):
            pool.memset(ident[:, :], 0.0).then_inc(pool_step, 1)
            pool.memset(causal[:, :], 0.0).then_inc(pool_step, 1)
            pool.wait_ge(pool_step, 2)
            pool.affine_select(out=ident[:, :], in_=ident[:, :], compare_op=ALU.not_equal, fill=1.0, base=0,
                               pattern=[[-1, P]], channel_multiplier=1).then_inc(const_ready, 1)
            pool.memset(ones[:, :], 1.0).then_inc(const_ready, 1)
            pool.memset(eps[:, :], EPS).then_inc(const_ready, 1)
            pool.memset(acc_init[:, :], 0.0).then_inc(const_ready, 1)
            pool.affine_select(out=causal[:, :], in_=causal[:, :], compare_op=ALU.is_ge, fill=MASKED, base=0,
                               pattern=[[-1, P]], channel_multiplier=1).then_inc(pool_step, 1)
            for row, v, tall in ((G_PRE_MIX, g_pre_mix, KT), (G_PRE_MLP, g_pre_mlp, KT), (CONVB, conv_b, CT), (B_RG, b_rg, CT),
                                 (B_IG, b_ig, CT), (LAMBDA, lru_lambda, CT), (G_LRU, g_lru_out, CT), (G_ATT, g_att_out, CT)):
                pool.dma_start(vrow[row:row + tall, :], v.rearrange("l (r n) -> (l r) n", n=P)).then_inc(vec_in, 16)
            pool.dma_start(vrow[CONVW:CONVW + CW * CT, :], conv_w.rearrange("l w (r n) -> (l w r) n", n=P)).then_inc(vec_in, 16)
            pool.dma_start(bf[:, :], b_forget.rearrange("l h -> h l")).then_inc(bf_in, 16)
            pool.dma_start(wf_raw[:, :, :], w_in2[:, 2 * D_LRU + 3 * D_ATT:].rearrange("(k p) n -> p k n", p=P)).then_inc(wf_in, 16)
            pool.wait_ge(x_ssq, NT)
            pool.memset(wrg[:, :, :], 0.0).then_inc(gw_zero, 1)
            pool.memset(wig[:, :, :], 0.0).then_inc(gw_zero, 1)
            for j in range(8):
                slot, _, s = unit(2 * j + 1)
                pool.wait_ge(hi_ready, 2 * j + 2)
                pool.tensor_tensor(w_lo[:, s], raw[:, slot], w_hi[:, s].bitcast(F32), ALU.subtract).then_inc(lo_pool, 1)
                for kt in (2 * j, 2 * j + 1):
                    pool.wait_ge(h_hi_ready, kt + 1)
                    pool.tensor_scalar(xnT[:, kt, :], xnT[:, kt, :], A1[:, kt:kt + 1], S1[:, kt:kt + 1], ALU.mult,
                                       ALU.add).then_inc(h_sum, 1)
                    pool.wait_ge(h_sum, kt + 1)
                    pool.tensor_tensor(h_lo[:, kt, :], xnT[:, kt, :], h_hi[:, kt, :].bitcast(F32), ALU.subtract).then_inc(h_lo_ready, 1)
            for ch in range(CT):
                pool.wait_ge(sig_done, 2 * ch + 2)
                pool.tensor_tensor(ig[:, ch, :], ig[:, ch, :], hs[:, ch, :], ALU.mult).then_inc(ix_ready, 1)
            for ch in range(CT):
                pool.wait_ge(y_done, ch + 1)
                if ch == 0:
                    pool.tensor_tensor(ssq[:, :], hs[:, ch, :], hs[:, ch, :], ALU.mult).then_inc(ssq_done, 1)
                else:
                    pool.wait_ge(ssq_done, ch)
                    pool.tensor_tensor(sq[:, :], hs[:, ch, :], hs[:, ch, :], ALU.mult).then_inc(pool_step, 1)
                    pool.wait_ge(pool_step, 3 + ch)
                    pool.tensor_tensor(ssq[:, :], ssq[:, :], sq[:, :], ALU.add).then_inc(ssq_done, 1)
            pool.wait_ge(ssq_done, CT)
            pool.memset(wf_hi[:, :, :].bitcast(F32), 0.0).then_inc(wf_zero, 1)
            pool.memset(wf_lo[:, :, :].bitcast(F32), 0.0).then_inc(wf_zero, 1)

            def load_nf(h):
                if h >= 2:
                    pool.wait_ge(neg_max, 4 * (h - 1))
                    pool.wait_ge(nfm_ready, h - 1)
                pool.dma_start(nF[:, h % 2, :], f_scr[h:h + 1, :].to_broadcast([P, S])).then_inc(nf_in[h % 2], 16)

            def mask_nf(h):
                pool.wait_ge(nf_in[h % 2], 16 * (h // 2 + 1))
                if h:
                    pool.wait_ge(neg_max, 4 * h)
                pool.tensor_tensor(nFm[:, :].rearrange("p (i k) -> p i k", k=P), nF[:, h % 2, :].rearrange("p (i k) -> p i k", k=P),
                                   causal[:, :].unsqueeze(1).to_broadcast([P, NT, P]), ALU.add).then_inc(nfm_ready, 1)

            pool.wait_ge(nf_ready, 1)
            pool.dma_start(f_scr[:, :], ut[0:HEADS, 7, :]).then_inc(nf_stored, 16)
            pool.wait_ge(nf_stored, 16)
            load_nf(0)
            load_nf(1)
            pool.wait_ge(pool_step, 2 + CT)
            mask_nf(0)
            for h in range(HEADS):
                if h + 1 < HEADS:
                    mask_nf(h + 1)
                if h + 2 < HEADS:
                    load_nf(h + 2)
                pool.wait_ge(ya_sq, h + 1)
                if h == 0:
                    pool.wait_ge(row_done, 1)
                    pool.tensor_copy(ssq[:, :], g_row[:, :]).then_inc(att_ssq, 1)
                else:
                    pool.wait_ge(att_ssq, h)
                    pool.tensor_tensor(ssq[:, :], ssq[:, :], g_row[:, :], ALU.add).then_inc(att_ssq, 1)

            def load_gain(q):
                pool.wait_ge(gate_ready, q) if q else pool.wait_ge(att_ssq, HEADS)
                g = (g_post_mix, g_post_mlp)[q // 4]
                pool.dma_start(g_row[:, :], g[0:1, q % 4 * COLS:(q % 4 + 1) * COLS].to_broadcast([P, COLS])).then_inc(gain_in, 16)

            def load_x(t):
                dst = xr2[:, :] if t == 2 else xr[:, t % 2, :]
                pool.dma_start(dst, x2[t * P:(t + 1) * P, :]).then_inc(xr_in[t], 16)

            load_gain(0)
            pool.wait_ge(pv_done, HEADS)
            load_x(2)
            load_gain(1)
            pool.wait_ge(y_sum, 8)
            load_x(0)
            load_x(1)
            for q in (2, 3, 4):
                load_gain(q)
            for t in range(NT):
                pool.wait_ge(x1_done, t + 1)
                pool.dma_start(x1_scr[t * P:(t + 1) * P, :], yg[:, t, :]).then_inc(x1_stored, 16)
                if t == 1:
                    load_x(3)
            for q in (5, 6, 7):
                load_gain(q)
            pool.wait_ge(x1_stored, 16 * NT)
            pool.wait_ge(unit_used, U_MLP + (CHUNKS - 1) * PER_CHUNK + 16)
            for t in range(NT):
                pool.dma_start(x1r[:, t, :], x1_scr[t * P:(t + 1) * P, :]).then_inc(x1r_in, 16)

    return nc


_INS = ['x', 'c', 'w_ada', 'b_ada', 'g_pre_mix', 'g_post_mix', 'g_pre_mlp', 'g_post_mlp', 'w_in', 'conv_w', 'conv_b',
        'w_rg', 'b_rg', 'w_ig', 'b_ig', 'lru_lambda', 'b_forget', 'g_lru_out', 'g_att_out', 'w_out', 'w_ff1', 'w_ff2']


def kernel(**inputs):
    import numpy as _np
    import concourse.bacc as _bacc
    from concourse import mybir as _mybir
    from concourse.bass_utils import run_bass_kernel_spmd as _run

    nc = _bacc.Bacc("TRN2", target_bir_lowering=False, num_devices=1)
    arrays, args = {}, []
    for name in _INS:
        a = _np.ascontiguousarray(inputs[name])
        arrays[f"in_{name}_dram"] = a
        args.append(nc.dram_tensor(f"in_{name}_dram", a.shape, _mybir.dt.from_np(a.dtype), kind="ExternalInput").ap())
    shape = tuple(inputs["x"].shape)
    args.append(nc.dram_tensor("out_0_dram", shape, _mybir.dt.float32, kind="ExternalOutput").ap())
    hybrid_layer(nc, *args)
    r = _run(nc, [arrays], core_ids=[0])
    return r.results[0]["out_0_dram"]
```
